# Optimizing a Trainium2 kernel written in Bass

```python
import jax, jax.numpy as jnp
from jax import lax
import numpy as np

D_MODEL = 1024
BATCH = 1
SEQ = 512
DEPTH = 2

CHUNK = 64
SC_WIDTH = D_MODEL // 2
SC_KERNEL = 3
GLA_HEADS = 4
GLA_DK = D_MODEL // 2 // GLA_HEADS
GLA_DV = D_MODEL // GLA_HEADS
GLA_RANK = 16
GLA_GATE_NORM = 16.0
CF_KERNEL = 31
MLP_HIDDEN = 4 * D_MODEL
EPS = 1e-6

GLA_KEY = GLA_HEADS * GLA_DK
GLA_VAL = GLA_HEADS * GLA_DV
AB_SPLIT = (SC_WIDTH, SC_WIDTH, SC_WIDTH, GLA_KEY, GLA_KEY, GLA_VAL, GLA_VAL, GLA_RANK)
AB_IN = sum(AB_SPLIT)
AB_MIX = SC_WIDTH + GLA_VAL

kernel_name = "hybrid_shortconv_gla_conformer_trunk"

def rms_norm(x, g):
    xf = x.astype(jnp.float32)
    y = xf * lax.rsqrt(jnp.mean(jnp.square(xf), axis=-1, keepdims=True) + EPS)
    return (y * g.astype(jnp.float32)).astype(x.dtype)

def layer_norm(x, g, b):
    xf = x.astype(jnp.float32)
    mu = jnp.mean(xf, axis=-1, keepdims=True)
    xc = xf - mu
    y = xc * lax.rsqrt(jnp.mean(jnp.square(xc), axis=-1, keepdims=True) + EPS)
    return (y * g.astype(jnp.float32) + b.astype(jnp.float32)).astype(x.dtype)

def causal_depthwise_conv(x, w):
    K, C = w.shape
    return lax.conv_general_dilated(
        x, w[:, None, :].astype(x.dtype), window_strides=(1,), padding=[(K - 1, 0)],
        dimension_numbers=('NWC', 'WIO', 'NWC'), feature_group_count=C)

def split_cols(z, sizes):
    idx, acc = [], 0
    for s in sizes[:-1]:
        acc += s
        idx.append(acc)
    return jnp.split(z, idx, axis=-1)

def gla_chunked(q, k, v, gk, g_out, norm_g):
    B, T, _ = q.shape
    N = T // CHUNK
    out_dtype = v.dtype

    def heads(t, d):
        return t.reshape(B, N, CHUNK, GLA_HEADS, d).transpose(1, 0, 3, 2, 4).astype(jnp.float32)

    qh = heads(q, GLA_DK) * (GLA_DK ** -0.5)
    kh = heads(k, GLA_DK)
    vh = heads(v, GLA_DV)
    gh = heads(jax.nn.log_sigmoid(gk.astype(jnp.float32)) / GLA_GATE_NORM, GLA_DK)
    causal = jnp.tril(jnp.ones((CHUNK, CHUNK), dtype=bool))[None, None, :, :, None]

    def body(S, inp):
        qc, kc, vc, gc = inp
        b = jnp.cumsum(gc, axis=2)
        b_last = b[:, :, -1, :]
        o_inter = jnp.einsum('bhik,bhkv->bhiv', qc * jnp.exp(b), S)
        diff = b[:, :, :, None, :] - b[:, :, None, :, :]
        decay = jnp.where(causal, jnp.exp(jnp.minimum(diff, 0.0)), 0.0)
        attn = jnp.einsum('bhik,bhijk,bhjk->bhij', qc, decay, kc)
        o = o_inter + jnp.einsum('bhij,bhjv->bhiv', attn, vc)
        S_new = S * jnp.exp(b_last)[..., None] + jnp.einsum(
            'bhjk,bhjv->bhkv', kc * jnp.exp(b_last[:, :, None, :] - b), vc)
        return S_new, o

    S0 = jnp.zeros((B, GLA_HEADS, GLA_DK, GLA_DV), jnp.float32)
    _, o = lax.scan(body, S0, (qh, kh, vh, gh))
    o = o.transpose(1, 0, 3, 2, 4).reshape(B, T, GLA_HEADS, GLA_DV)
    o = rms_norm(o, norm_g) * jax.nn.silu(g_out.astype(jnp.float32).reshape(B, T, GLA_HEADS, GLA_DV))
    return o.reshape(B, T, GLA_VAL).astype(out_dtype)

def shortconv_gla_mixer(h, w_in, w_gk2, b_gk2, w_sc, gla_norm_g, w_out):
    z = h @ w_in
    sc_x, sc_b, sc_c, q, k, v, g_out, gk_lr = split_cols(z, AB_SPLIT)
    y_a = sc_b * causal_depthwise_conv(sc_c * sc_x, w_sc)
    gk = gk_lr @ w_gk2 + b_gk2
    y_b = gla_chunked(q, k, v, gk, g_out, gla_norm_g)
    return jnp.concatenate([y_a, y_b], axis=-1) @ w_out

def conformer_conv(h, w_pw1, b_pw1, w_dw, b_dw, ln_g, ln_b, w_pw2, b_pw2):
    u = h @ w_pw1 + b_pw1
    u1, u2 = jnp.split(u, 2, axis=-1)
    u = u1 * jax.nn.sigmoid(u2)
    d = causal_depthwise_conv(u, w_dw) + b_dw
    d = jax.nn.silu(layer_norm(d, ln_g, ln_b))
    return d @ w_pw2 + b_pw2

def setup_inputs(seed: int = 0) -> dict:
    key = jax.random.key(seed)
    ks = iter(jax.random.split(key, 32))
    ne = (DEPTH + 1) // 2
    no = DEPTH // 2
    D = D_MODEL

    def nrm(shape, scale):
        return jax.random.normal(next(ks), shape, jnp.float32) * scale

    def gain(shape):
        return 1.0 + nrm(shape, 0.02)

    return {
        "x": nrm((BATCH, SEQ, D), 1.0),
        "norm_mix_pre": gain((DEPTH, D)),
        "norm_mix_post": gain((DEPTH, D)),
        "norm_mlp_pre": gain((DEPTH, D)),
        "norm_mlp_post": gain((DEPTH, D)),
        "ab_w_in": nrm((ne, D, AB_IN), D ** -0.5),
        "gla_w_gk2": nrm((ne, GLA_RANK, GLA_KEY), GLA_RANK ** -0.5),
        "gla_b_gk2": nrm((ne, GLA_KEY), 0.01),
        "sc_w_conv": nrm((ne, SC_KERNEL, SC_WIDTH), SC_KERNEL ** -0.5),
        "gla_norm_g": gain((ne, GLA_DV)),
        "ab_w_out": nrm((ne, AB_MIX, D), AB_MIX ** -0.5),
        "cf_w_pw1": nrm((no, D, 2 * D), D ** -0.5),
        "cf_b_pw1": nrm((no, 2 * D), 0.01),
        "cf_w_dw": nrm((no, CF_KERNEL, D), CF_KERNEL ** -0.5),
        "cf_b_dw": nrm((no, D), 0.01),
        "cf_ln_g": gain((no, D)),
        "cf_ln_b": nrm((no, D), 0.01),
        "cf_w_pw2": nrm((no, D, D), D ** -0.5),
        "cf_b_pw2": nrm((no, D), 0.01),
        "mlp_w1": nrm((DEPTH, D, MLP_HIDDEN), D ** -0.5),
        "mlp_w2": nrm((DEPTH, MLP_HIDDEN, D), MLP_HIDDEN ** -0.5),
    }

def reference(x, norm_mix_pre, norm_mix_post, norm_mlp_pre, norm_mlp_post,
              ab_w_in, gla_w_gk2, gla_b_gk2, sc_w_conv, gla_norm_g, ab_w_out,
              cf_w_pw1, cf_b_pw1, cf_w_dw, cf_b_dw, cf_ln_g, cf_ln_b, cf_w_pw2, cf_b_pw2,
              mlp_w1, mlp_w2):
    for layer in range(DEPTH):
        i = layer // 2
        h = rms_norm(x, norm_mix_pre[layer])
        if layer % 2 == 0:
            y = shortconv_gla_mixer(h, ab_w_in[i], gla_w_gk2[i], gla_b_gk2[i],
                                    sc_w_conv[i], gla_norm_g[i], ab_w_out[i])
        else:
            y = conformer_conv(h, cf_w_pw1[i], cf_b_pw1[i], cf_w_dw[i], cf_b_dw[i],
                               cf_ln_g[i], cf_ln_b[i], cf_w_pw2[i], cf_b_pw2[i])
        x = x + rms_norm(y, norm_mix_post[layer])
        h = rms_norm(x, norm_mlp_pre[layer])
        y = jnp.square(jax.nn.relu(h @ mlp_w1[layer])) @ mlp_w2[layer]
        x = x + rms_norm(y, norm_mlp_post[layer])
    return x


_drawn_inputs = setup_inputs


def setup_inputs(seed=0):
    import zlib

    import numpy as np

    out = dict(_drawn_inputs(seed))
    spreads = {}
    factors = {'norm_mix_post': 2.914,
     'norm_mlp_pre': 3.347,
     'norm_mlp_post': 10.866,
     'gla_b_gk2': 8.0,
     'gla_norm_g': 5.177,
     'cf_b_pw1': 8.0,
     'cf_b_dw': 5.486,
     'cf_ln_g': 24.762,
     'cf_ln_b': 49.831,
     'cf_b_pw2': 35.471}
    for name, (base, spread) in spreads.items():
        noise = np.random.default_rng([zlib.crc32(name.encode()), seed]).standard_normal(out[name].shape)
        drawn = base * np.exp(spread * noise) if base else spread * noise
        out[name] = __import__('jax').numpy.asarray(drawn.astype(out[name].dtype))
    for name, factor in factors.items():
        out[name] = (out[name] * factor).astype(out[name].dtype)
    return out
```

```python
from contextlib import ExitStack

import concourse.bass as bass
import numpy as np
from concourse import mybir

P = 128
D = 1024
T = 512
KT = D // P
CHUNK = 64
HEADS = 4
DK = D // 2 // HEADS
DV = D // HEADS
RANK = 16
SCW = D // 2
GATE_NORM = 16.0
CF_K = 31
HID = 4 * D
HT = HID // P
EPS = 1e-6
CP = T // P
LEVELS = 6

VEC_SIZES = [("mix_pre", 2 * KT), ("mix_post", 2 * KT), ("mlp_pre", 2 * KT), ("mlp_post", 2 * KT),
             ("b_pw1", 2 * KT), ("b_dw", KT), ("ln_g", KT), ("ln_b", KT), ("b_pw2", KT),
             ("gla_g", DV // P), ("w_sc", 3 * SCW // P), ("w_dw", CF_K * KT), ("eps", 1), ("zero", 1)]
VEC, _at = {}, 0
for _name, _n in VEC_SIZES:
    VEC[_name] = _at
    _at += _n
NVEC = _at

STAGES = [("in_proj", 36), ("out_proj", 12), ("up0", 32), ("down0", 32), ("pw1", 16), ("pw2", 8),
          ("up1", 32), ("down1", 32)]
FIRST, _at = {}, 0
for _name, _n in STAGES:
    FIRST[_name] = _at
    _at += _n
STEPS = dict(STAGES)
TOTAL_STEPS = _at
RING = 4
AHEAD = 3


def build(nc, x_t, w_in, w_gk2, b_gk2, w_out, w_pw1, w_pw2, w_up, w_down, vecs, squares, masks, out_t):
    fp32, f32r, u8 = mybir.dt.float32, mybir.dt.float32r, mybir.dt.uint8
    ALU, ACT = mybir.AluOpType, mybir.ActivationFunctionType
    ctx = ExitStack()
    with ctx:
        def sb(name, shape, dt=fp32):
            return ctx.enter_context(nc.sbuf_tensor(name, shape, dt))

        def sem(name):
            return ctx.enter_context(nc.semaphore(name))

        x = sb("x", [P, KT, T])
        raw = [sb(f"raw{i}", [P, D]) for i in range(RING)]
        w_hi = [sb(f"w_hi{i}", [P, D], f32r) for i in range(RING)]
        w_lo = [sb(f"w_lo{i}", [P, D], f32r) for i in range(RING)]
        h_hi = sb("h_hi", [P, KT, T], f32r)
        h_lo = sb("h_lo", [P, KT, T], f32r)
        y = sb("y", [P, KT, T])
        vec = sb("vec", [P, NVEC])
        sq_const = sb("sq_const", [P, 3, P])
        mask = sb("mask", [P, LEVELS * CHUNK + P], u8)
        acc = sb("acc", [P, T])
        work = [sb(f"work{i}", [P, T]) for i in range(2)]
        rs = sb("rs", [P, T])
        rs_tok = sb("rs_tok", [P, CP])
        e_last = sb("e_last", [P, HEADS, T // CHUNK])
        w_lr = sb("w_lr", [P, KT, RANK])
        with nc.sbuf_tensor("gate", [P, 2 * HEADS, T], fp32) as gate:
            pass
        m_hl = sb("m_hl", [P, RING, 2, T], f32r)
        with ExitStack() as over:
            def mx(name, shape):
                return over.enter_context(nc.sbuf_tensor(name, shape, fp32))
            y_a = mx("y_a", [P, SCW // P, T])
            o = mx("o", [P, 2 * HEADS, T])
            q = mx("q", [P, HEADS, T])
            k = mx("k", [P, HEADS, T])
            b = mx("b", [P, HEADS, T])
            v = mx("v", [P, CP, HEADS * DV])
        with ExitStack() as over:
            def mx(name, shape):
                return over.enter_context(nc.sbuf_tensor(name, shape, fp32))
            u = mx("u", [P, KT, CF_K - 1 + T])
            d = mx("d", [P, KT, T])
            sg = mx("sg", [P, 4, T])
            act_d = mx("act_d", [P, KT, T])
        mid = sb("mid", [P, HT, T])

        scores = x[:, 0:4, :].rearrange("p a (c i) -> p (a c) i", i=P)
        q_lv = x[:, 4:6, :].rearrange("p a n -> p (a n)")
        e_lv = o[:, 0:4, :].rearrange("p a n -> p (a n)")
        k_lv = o[:, 4:8, :]
        g_tok = o[:, 0:4, :]
        softp = o[:, 4:8, :]
        kd_tok = b
        sc_p = k
        lr = y[0:RANK + 1, 0, :]
        wgk2 = y[0:RANK + 1, 1, :]
        mask_in = y[:, 2, :]
        states = y[:, :, :].rearrange("p (s a) n -> p s (a n)", s=RING)
        ones = sq_const[:, 0, :]
        ident = sq_const[:, 1, :]
        tri = sq_const[:, 2, :]

        ps = ctx.enter_context(nc.psum_tensor("ps", [P, 8, 512], fp32))

        def vcol(name, c):
            return vec[:, VEC[name] + c:VEC[name] + c + 1]

        eps = vcol("eps", 0)

        s_const = sem("s_const")
        s_lr_in = sem("s_lr_in")
        s_gk_in = sem("s_gk_in")
        s_x = [sem(f"s_x{i}") for i in range(KT)]
        s_x_again = sem("s_x_again")
        s_raw = [sem(f"s_raw{i}") for i in range(RING)]
        s_whi = sem("s_whi")
        s_wlo = sem("s_wlo")
        s_pe = {n: sem(f"s_pe_{n}") for n, _ in STAGES}
        s_free = sem("s_free")
        s_hhi = sem("s_hhi")
        s_hlo = sem("s_hlo")
        s_xsq = sem("s_xsq")
        s_acc = sem("s_acc")
        s_ss = sem("s_ss")
        s_sqrt = sem("s_sqrt")
        s_rs = sem("s_rs")
        s_mid = sem("s_mid")
        s_mhi = sem("s_mhi")
        s_mlo = sem("s_mlo")
        s_yn = sem("s_yn")
        s_xnew = sem("s_xnew")
        s_out = sem("s_out")
        s_set = sem("s_set")
        s_lrp = sem("s_lrp")
        s_lr = sem("s_lr")
        s_gkp = sem("s_gkp")
        s_sp = sem("s_sp")
        s_g = sem("s_g")
        s_bp = sem("s_bp")
        s_b = sem("s_b")
        s_e = sem("s_e")
        s_exp = sem("s_exp")
        s_qk = sem("s_qk")
        s_sc = sem("s_sc")
        s_pred = sem("s_pred")
        s_kdp = sem("s_kdp")
        s_kd = sem("s_kd")
        s_el = sem("s_el")
        s_u = sem("s_u")
        s_state = sem("s_state")
        s_op = sem("s_op")
        s_o = sem("s_o")
        s_osq = sem("s_osq")
        s_oadd = sem("s_oadd")
        s_oss = sem("s_oss")
        s_osqrt = sem("s_osqrt")
        s_ors = sem("s_ors")
        s_silu = sem("s_silu")
        s_scv = sem("s_scv")
        s_sig = sem("s_sig")
        s_uw = sem("s_uw")
        s_u1 = sem("s_u1")
        s_cv = sem("s_cv")
        s_lnsq = sem("s_lnsq")
        s_lnadd = sem("s_lnadd")
        s_lnroot = sem("s_lnroot")
        s_lnrs = sem("s_lnrs")
        s_ln = sem("s_ln")
        s_lnp = sem("s_lnp")
        s_z = sem("s_z")

        block = ctx.enter_context(nc.Block())

        def narrow_step_done(step):
            g, j = divmod(step, 4)
            return 7 * g + (j + 1 if j < 3 else 7)

        def narrow_bank_done(g, m):
            return 7 * g + 3 + m + 1

        def wide_bank_done(stage, m):
            return STEPS[stage] - 1 + m + 1

        FREED = {"in_proj": 0, "out_proj": 36, "up0": 44, "down0": 76, "pw1": 84, "pw2": 100,
                 "up1": 108, "down1": 140}
        WIDE = ("out_proj", "down0", "pw2", "down1")
        ORDER = [n for n, _ in STAGES]

        @block.sync
        def _(sp):
            def narrow_group(w, g0, col, i=None, n=0):
                for j in range(4):
                    step = g0 + j if i is None else None
                    src = w[256 * j:256 * j + 256, bass.ds(col, 512)].rearrange("(a p) n -> p a n", p=P)
                    if i is None:
                        if step >= RING:
                            sp.wait_ge(s_wlo, step - RING + 1)
                    else:
                        sp.wait_ge(s_wlo, i * n + (g0 + j - RING + 1))
                    sp.dma_start(raw[j][:, :].rearrange("p (a n) -> p a n", a=2), src).then_inc(s_raw[j], 16)

            sp.dma_start(vec[:, :], vecs).then_inc(s_const, 16)
            sp.dma_start(x[:, 0, :], x_t[0:P, :]).then_inc(s_x[0], 16)
            cols = [1536, 2048, 2560, 3072, 3584, 4096, 0, 1024, 512]
            narrow_group(w_in, 0, cols[0])
            sp.dma_start(sq_const[:, :, :], squares).then_inc(s_const, 16)
            sp.dma_start(mask_in, masks).then_inc(s_const, 16)
            sp.dma_start(w_lr[:, :, :], w_in[:, 4608:4624].rearrange("(a p) n -> p a n", p=P)).then_inc(s_lr_in, 16)
            sp.dma_start(wgk2[0:RANK, :], w_gk2).then_inc(s_gk_in, 16)
            sp.dma_start(wgk2[RANK:RANK + 1, :], b_gk2).then_inc(s_gk_in, 16)
            for g in range(1, 9):
                narrow_group(w_in, 4 * g, cols[g])

            def wide(stage, w, row0, k0, k1):
                base = FIRST[stage]
                with sp.Fori(k0 // 4, k1 // 4) as i:
                    for s in range(4):
                        row = sp.snap(i * 512 + (row0 + s * P))
                        sp.wait_ge(s_wlo, i * 4 + (base + s - RING + 1))
                        sp.dma_start(raw[s][:, :], w[bass.ds(row, P), :]).then_inc(s_raw[s], 16)

            wide("out_proj", w_out, SCW, 0, 8)
            wide("out_proj", w_out, -8 * P, 8, 12)
            sp.wait_ge(s_op, CP)
            sp.dma_start(x[:, :, :], x_t.rearrange("(a p) n -> p a n", p=P)).then_inc(s_x_again, 16)

            def mlp(layer):
                with sp.Fori(0, 8) as i:
                    col = sp.snap(i * 512)
                    narrow_group(w_up[layer], FIRST[f"up{layer}"], col, i, 4)
                wide(f"down{layer}", w_down[layer], 0, 0, HT)

            mlp(0)
            for g, c in enumerate((1024, 0, 1536, 512)):
                narrow_group(w_pw1, FIRST["pw1"] + 4 * g, c)
            wide("pw2", w_pw2, 0, 0, KT)
            mlp(1)
            for m in range(KT):
                sp.wait_ge(s_xnew, 3 * KT + m + 1)
                sp.dma_start(out_t[m * P:(m + 1) * P, :], x[:, m, :]).then_inc(s_out, 16)
            sp.wait_ge(s_out, 16 * KT)

        @block.gpsimd
        def _(pool):
            with pool.Fori(0, TOTAL_STEPS // RING) as i:
                for s in range(RING):
                    pool.wait_ge(s_whi, i * RING + (s + 1))
                    nc.gpsimd.tensor_tensor(w_lo[s][:, :], raw[s][:, :], w_hi[s][:, :].bitcast(fp32),
                                            ALU.subtract).then_inc(s_wlo, 1)

        @block.scalar
        def _(act):
            def w_high(step):
                s = step % RING
                act.wait_ge(s_raw[s], 16 * (step // RING + 1))
                if step >= RING:
                    free = step - RING
                    stage = [n for n in ORDER if FIRST[n] <= free][-1]
                    local = free - FIRST[stage]
                    last = local == STEPS[stage] - 1
                    done = narrow_step_done(local) if stage not in WIDE else (
                        wide_bank_done(stage, 7) if last else local + 1)
                    act.wait_ge(s_pe[stage], done)
                nc.scalar.activation(w_hi[s][:, :], raw[s][:, :], ACT.Copy).then_inc(s_whi, 1)

            def m_high(src, kk, ready, slot_free):
                if ready is not None:
                    act.wait_ge(*ready)
                if slot_free is not None:
                    act.wait_ge(*slot_free)
                nc.scalar.activation(m_hl[:, kk % RING, 0, :], src, ACT.Copy).then_inc(s_mhi, 1)

            for m in range(1, KT):
                act.dma_start(x[:, m, :], x_t[m * P:(m + 1) * P, :]).then_inc(s_x[m], 16)
            act.wait_ge(s_const, 48)

            def open_tile(m, o_idx, gain, ready):
                act.wait_ge(*ready)
                nc.scalar.activation(h_hi[:, m, :], x[:, m, :], ACT.Copy, scale=gain).then_inc(s_hhi, 1)
                square_tile(m, 2 * o_idx, x)

            def square_tile(m, norm, src):
                if m >= 3:
                    act.wait_ge(s_acc, 7 * norm + m - 2)
                dst = acc if m == 0 else work[m % 2]
                nc.scalar.activation(dst[:, :], src[:, m, :], ACT.Square).then_inc(s_xsq, 1)

            for m in range(KT):
                if m < 3:
                    w_high(m)
                open_tile(m, 0, vcol("mix_pre", m), (s_x[m], 16))

            def root(norm, bank):
                act.wait_ge(s_ss, norm + 1)
                nc.scalar.activation(rs[:, :], ps[:, bank, :], ACT.Sqrt, bias=eps, scale=1.0 / D).then_inc(s_sqrt, 1)

            for n in range(36):
                w_high(n + AHEAD)
                if n == 4:
                    root(0, 7)
                    nc.scalar.activation(rs_tok[:, :], ps[:, 6, 0:CP], ACT.Sqrt, bias=eps, scale=1.0 / D).then_inc(s_sqrt, 1)
                if n == 7:
                    act.wait_ge(s_gkp, 1)
                    nc.scalar.activation(softp, ps[:, 4:8, :], ACT.Abs).then_inc(s_sp, 1)
                    act.wait_ge(s_sp, 1)
                    nc.scalar.activation(softp, softp, ACT.Exp, scale=-1.0).then_inc(s_sp, 1)
                    act.wait_ge(s_sp, 2)
                    nc.scalar.activation(softp, softp, ACT.Ln, bias=1.0).then_inc(s_sp, 1)
                if n == 10:
                    act.wait_ge(s_bp, 1)
                    nc.scalar.activation(b[:, :, :], ps[:, 4:8, :], ACT.Copy).then_inc(s_b, 1)
                if 13 <= n < 13 + LEVELS:
                    act.wait_ge(s_e, 2 * (n - 13) + 2)
                    nc.scalar.activation(e_lv, e_lv, ACT.Exp).then_inc(s_exp, 1)
                if n == 19:
                    act.wait_ge(s_qk, 2 * LEVELS)
                    nc.scalar.activation(e_lv, b[:, :, :].rearrange("p a n -> p (a n)"), ACT.Exp).then_inc(s_exp, 1)
                    nc.scalar.activation(e_last[:, :, :], b[:, :, CHUNK - 1::CHUNK], ACT.Exp).then_inc(s_el, 1)
                if n == 20:
                    act.wait_ge(s_e, 2 * LEVELS + 1)
                    nc.scalar.activation(e_lv, e_lv, ACT.Exp).then_inc(s_exp, 1)
                if n == 22:
                    act.wait_ge(s_kdp, 1)
                    nc.scalar.activation(kd_tok[:, :, :], ps[:, 4:8, :], ACT.Copy).then_inc(s_kd, 1)
                if n in (21, 25):
                    for t in range(4):
                        c = t + (4 if n == 25 else 0)
                        act.wait_ge(s_free, 16 + c + 1)
                        nc.scalar.activation(gate[:, c, :], gate[:, c, :], ACT.Silu).then_inc(s_silu, 1)
                if n in (25, 27, 29, 31):
                    c = (n - 25) // 2
                    act.wait_ge(s_op, c + 1)
                    nc.scalar.activation(o[:, :, c * P:(c + 1) * P],
                                         ps[:, 4:6, :].rearrange("p a (c n) -> p (a c) n", n=P), ACT.Copy).then_inc(s_o, 1)
                if n == 32:
                    act.wait_ge(s_o, CP)
                    osq = v[:, :, :].rearrange("p a (c n) -> p (a c) n", n=T)
                    nc.scalar.activation(osq[:, 0:4, :], o[:, 0:4, :], ACT.Square).then_inc(s_osq, 1)
                    nc.scalar.activation(osq[:, 4:8, :], o[:, 4:8, :], ACT.Square).then_inc(s_osq, 1)
                if n == 34:
                    act.wait_ge(s_oss, 1)
                    nc.scalar.activation(q[:, :, :], ps[:, 4:8, :], ACT.Sqrt, bias=eps, scale=1.0 / DV).then_inc(s_osqrt, 1)

            def wide_stage(stage, tiles, mid0, ready, first=0):
                base = FIRST[stage]
                for kk in range(first, 3):
                    m_high(tiles(kk), mid0 + kk, ready(kk), None)
                n = len_of = STEPS[stage]
                for kk in range(n):
                    if base + kk + AHEAD < TOTAL_STEPS:
                        w_high(base + kk + AHEAD)
                    if kk + 3 < n:
                        m_high(tiles(kk + 3), mid0 + kk + 3, ready(kk + 3), (s_pe[stage], kk) if kk else None)

            def close(stage, o_idx, pre):
                post = 2 * o_idx - 1
                for m in range(KT):
                    act.wait_ge(s_free, FREED[stage] + m + 1)
                    square_tile(m, post, y)
                root(post, 0)
                if pre:
                    for m in range(KT):
                        open_tile(m, o_idx, vcol(pre[0], pre[1] + m), (s_xnew, KT * (o_idx - 1) + m + 1))

            out_tiles = [o[:, c, :] for c in range(8)] + [y_a[:, c, :] for c in range(4)]
            wide_stage("out_proj", lambda kk: out_tiles[kk], 0,
                       lambda kk: (s_mid, 2) if kk < 8 else (s_mid, 2 + kk - 7))
            close("out_proj", 1, ("mlp_pre", 0))

            def mlp(layer):
                up, down = f"up{layer}", f"down{layer}"
                o_idx = 1 if layer == 0 else 3
                mid_done = 6 if layer == 0 else 6 + HT + KT
                mhi0 = 12 if layer == 0 else 12 + HT + KT
                u0, d0 = FIRST[up], FIRST[down]
                for n in range(8):
                    w_high(u0 + n + AHEAD)
                    if n == 4:
                        root(2 * o_idx, 7)
                for kk in range(3):
                    m_high(mid[:, kk, :], kk, (s_mid, mid_done + kk + 1), None)
                with act.Fori(1, 4) as i:
                    for n in range(8):
                        s = (n + AHEAD) % RING
                        act.wait_ge(s_raw[s], i * 32 + 16 * ((u0 + n + AHEAD) // RING + 1))
                        if n == 0:
                            act.wait_ge(s_pe[up], i * 14)
                        else:
                            act.wait_ge(s_pe[up], i * 14 + narrow_step_done(n - 1))
                        nc.scalar.activation(w_hi[s][:, :], raw[s][:, :], ACT.Copy).then_inc(s_whi, 1)
                for kk in range(4):
                    w_high(d0 + kk + AHEAD)
                    m_high(mid[:, kk + 3, :], kk + 3, (s_mid, mid_done + kk + 4), (s_pe[down], kk) if kk else None)
                with act.Fori(1, 7) as i:
                    for c in range(4):
                        s = (c + AHEAD) % RING
                        act.wait_ge(s_raw[s], i * 16 + 16 * ((d0 + c + AHEAD) // RING + 1))
                        act.wait_ge(s_pe[down], i * 4 + c)
                        nc.scalar.activation(w_hi[s][:, :], raw[s][:, :], ACT.Copy).then_inc(s_whi, 1)
                        act.wait_ge(s_mid, i * 4 + (mid_done + c + 4))
                        nc.scalar.activation(m_hl[:, s, 0, :], mid[:, bass.ds(i * 4 + (c + 3), 1), :].rearrange("p a n -> p (a n)"),
                                             ACT.Copy).then_inc(s_mhi, 1)
                for kk in range(28, 32):
                    if d0 + kk + AHEAD < TOTAL_STEPS:
                        w_high(d0 + kk + AHEAD)
                    if kk + 3 < HT:
                        m_high(mid[:, kk + 3, :], kk + 3, (s_mid, mid_done + kk + 4), (s_pe[down], kk))
                close(down, o_idx + 1, ("mix_pre", KT) if layer == 0 else None)

            mlp(0)

            p0 = FIRST["pw1"]
            for n in range(16):
                w_high(p0 + n + AHEAD)
                if n == 4:
                    root(4, 7)
                if n in (5, 13):
                    for t in range(4):
                        c = t + (4 if n == 13 else 0)
                        act.wait_ge(s_free, FREED["pw1"] + 8 * (c // 4) + t + 1)
                        nc.scalar.activation(sg[:, t, :], sg[:, t, :], ACT.Sigmoid, bias=vcol("b_pw1", KT + c)).then_inc(s_sig, 1)
            for m in range(KT):
                act.wait_ge(s_ln, m + 1)
                if m >= 3:
                    act.wait_ge(s_lnadd, m - 2)
                nc.scalar.activation((acc if m == 0 else work[m % 2])[:, :], d[:, m, :], ACT.Square).then_inc(s_lnsq, 1)
            act.wait_ge(s_lnp, 2)
            nc.scalar.activation(rs[:, :], ps[:, 1, :], ACT.Sqrt, bias=eps, scale=1.0 / D).then_inc(s_lnroot, 1)

            def silu_tile(m):
                act.wait_ge(s_z, m + 1)
                nc.scalar.activation(act_d[:, m, :], d[:, m, :], ACT.Silu, bias=vcol("ln_b", m),
                                     scale=vcol("ln_g", m)).then_inc(s_mid, 1)

            mid0 = 6 + HT
            for m in range(3):
                silu_tile(m)
                m_high(act_d[:, m, :], m, (s_mid, mid0 + m + 1), None)
            q0 = FIRST["pw2"]
            for kk in range(KT):
                w_high(q0 + kk + AHEAD)
                if kk + 3 < KT:
                    silu_tile(kk + 3)
                    m_high(act_d[:, kk + 3, :], kk + 3, (s_mid, mid0 + kk + 4), (s_pe["pw2"], kk) if kk else None)
            close("pw2", 3, ("mlp_pre", KT))
            mlp(1)

        @block.tensor
        def _(pe):
            PASSES = ((0, 0), (1, 0), (0, 1))

            def h(kk, part):
                return (h_hi, h_lo)[part][:, kk, :]

            def wt(s, part, c, n=P):
                return (w_hi, w_lo)[part][s][:, c:c + n]

            def narrow_group(stage, g, bank0, step_of, bank_free, tokens_out=False, after=None, opening=None):
                for j in range(4):
                    pe.wait_ge(s_wlo, step_of(j))
                    for kk in (2 * j, 2 * j + 1):
                        if opening is not None:
                            pe.wait_ge(s_hhi, KT * opening + kk + 1)
                            pe.wait_ge(s_hlo, KT * opening + kk + 1)
                        for m in range(4):
                            if kk == 0:
                                free = bank_free(m)
                                if free is not None:
                                    pe.wait_ge(s_free, free)
                            c = (kk % 2) * 512
                            for n, (wp, hp) in enumerate(PASSES):
                                if tokens_out:
                                    lhs, rhs = h(kk, hp)[:, m * P:(m + 1) * P], wt(j, wp, c, 512)
                                else:
                                    lhs, rhs = wt(j, wp, c + m * P), h(kk, hp)
                                last = nc.tensor.matmul(ps[:, bank0 + m, :], lhs, rhs,
                                                        start=(kk == 0 and n == 0), stop=(kk == KT - 1 and n == 2))
                            if kk == KT - 1:
                                last.then_inc(s_pe[stage], 1)
                    if j < 3:
                        last.then_inc(s_pe[stage], 1)
                    if after is not None:
                        after(4 * g + j)

            def feature_sum(norm, bank):
                pe.wait_ge(s_acc, 7 * (norm + 1))
                nc.tensor.matmul(ps[:, bank, :], ones, acc[:, :], start=True, stop=True).then_inc(s_ss, 1)

            def gla(n):
                if n == 3:
                    pe.wait_ge(s_acc, 7)
                    for t in range(CP):
                        nc.tensor.matmul(ps[:, 6, t:t + 1], acc[:, t * P:(t + 1) * P], ones[:, 0:1], start=True, stop=True)
                    nc.tensor.matmul(ps[:, 7, :], ones, acc[:, :], start=True, stop=True).then_inc(s_ss, 1)
                if n == 4:
                    pe.wait_ge(s_set, 2)
                    for kk in range(KT):
                        last = nc.tensor.matmul(ps[0:RANK, 4, :], w_lr[:, kk, :], x[:, kk, :], start=(kk == 0), stop=(kk == KT - 1))
                    last.then_inc(s_lrp, 1)
                if n == 6:
                    pe.wait_ge(s_lr, 1)
                    pe.wait_ge(s_gk_in, 32)
                    pe.wait_ge(s_sqrt, 2)
                    for t in range(CP):
                        last = nc.tensor.matmul(ps[:, 4 + t, :], lr[:, t * P:(t + 1) * P], wgk2, start=True, stop=True)
                    last.then_inc(s_gkp, 1)
                if n == 9:
                    pe.wait_ge(s_g, CP)
                    for hd in range(HEADS):
                        for t in range(CP):
                            last = nc.tensor.matmul(ps[:, 4 + hd, t * P:(t + 1) * P], g_tok[:, t, hd * P:(hd + 1) * P], tri,
                                                    start=True, stop=True)
                    last.then_inc(s_bp, 1)
                if n in (11, 12):
                    half = n - 11
                    pe.wait_ge(s_b, 1)
                    pe.wait_ge(s_free, 8)
                    for hd in (2 * half, 2 * half + 1):
                        for c in range(CP):
                            last = nc.tensor.matmul(ps[:, 4 + hd, c * P:(c + 1) * P], k[:, hd, c * P:(c + 1) * P],
                                                    q[:, hd, c * P:(c + 1) * P], start=True, stop=True)
                    last.then_inc(s_sc, 1)
                if 14 <= n < 14 + LEVELS:
                    lv = n - 14
                    pe.wait_ge(s_qk, 2 * lv + 2)
                    pe.wait_ge(s_pred, lv + 2)
                    for hd in range(HEADS):
                        for c in range(CP):
                            at = (hd * CP + c) * CHUNK
                            last = nc.tensor.matmul(ps[:, 4 + 2 * (lv % 2) + hd // 2, at % 512:at % 512 + CHUNK],
                                                    k_lv[:, hd, c * P:(c + 1) * P], q_lv[:, at:at + CHUNK],
                                                    start=True, stop=True)
                    last.then_inc(s_sc, 1)
                if n == 21:
                    pe.wait_ge(s_qk, 2 * LEVELS + 2)
                    pe.wait_ge(s_pred, LEVELS + 3)
                    for c in range(CP):
                        for hd in range(HEADS):
                            last = nc.tensor.transpose(ps[:, 4 + c, hd * P:(hd + 1) * P], k[:, hd, c * P:(c + 1) * P], ident)
                    last.then_inc(s_kdp, 1)

                def chunk_update(c):
                    if c == 0:
                        pe.wait_ge(s_kd, 1)
                        pe.wait_ge(s_free, 16)
                    else:
                        pe.wait_ge(s_state, HEADS * c)
                    r = slice((c % 2) * CHUNK, (c % 2 + 1) * CHUNK)
                    for hd in range(HEADS):
                        at = hd * DV
                        last = nc.tensor.matmul(ps[:, 6 + hd // 2, at % 512:at % 512 + DV], kd_tok[r, c // 2, hd * P:(hd + 1) * P],
                                                v[r, c // 2, at:at + DV], start=True, stop=True)
                    last.then_inc(s_u, 1)

                def outputs(c):
                    if c == 0:
                        pe.wait_ge(s_kd, 1)
                    else:
                        pe.wait_ge(s_o, c)
                    pe.wait_ge(s_state, HEADS * (2 * c + 1))
                    for hd in range(HEADS):
                        for w in range(2):
                            at = (2 * hd + w) * P
                            bank, at = 4 + at // 512, at % 512
                            col = hd * DV + w * P
                            for ch in (2 * c, 2 * c + 1):
                                off = (ch % 2) * CHUNK
                                last = nc.tensor.matmul(ps[:, bank, at + off:at + off + CHUNK], v[:, c, col:col + P],
                                                        scores[:, hd * CP + c, off:off + CHUNK], start=True, stop=(ch == 0))
                                if ch:
                                    last = nc.tensor.matmul(ps[:, bank, at + off:at + off + CHUNK], states[:, ch % RING, col:col + P],
                                                            q[:, hd, ch * CHUNK:(ch + 1) * CHUNK], start=False, stop=True)
                    last.then_inc(s_op, 1)

                if n in (22, 23, 25, 27):
                    chunk_update(n - 22)
                if n in (24, 26, 28):
                    outputs((n - 24) // 2)
                    chunk_update(n - 22)
                if n == 30:
                    outputs(3)
                if n == 33:
                    pe.wait_ge(s_oadd, 1)
                    for hd in range(HEADS):
                        last = nc.tensor.matmul(ps[:, 4 + hd, :], ones, b[:, hd, :], start=True, stop=True)
                    last.then_inc(s_oss, 1)

            pe.wait_ge(s_const, 48)
            for g in range(9):
                narrow_group("in_proj", g, 0, lambda j: 4 * g + j + 1, lambda m: 4 * (g - 1) + m + 1 if g else None,
                             tokens_out=g in (2, 3), after=gla, opening=0 if g == 0 else None)

            def wide_block(stage, k0, banks_free, mlo0, i=None, start=False, stop=False):
                base = FIRST[stage]
                for c in range(4):
                    if i is None:
                        pe.wait_ge(s_wlo, base + k0 + c + 1)
                        pe.wait_ge(s_mlo, mlo0 + k0 + c + 1)
                    else:
                        pe.wait_ge(s_wlo, i * 4 + (base + c + 1))
                        pe.wait_ge(s_mlo, i * 4 + (mlo0 + c + 1))
                    for m in range(8):
                        if start and c == 0 and banks_free(m) is not None:
                            pe.wait_ge(s_free, banks_free(m))
                        for n, (wp, hp) in enumerate(PASSES):
                            last = nc.tensor.matmul(ps[:, m, :], wt(c, wp, m * P), m_hl[:, c, hp, :],
                                                    start=(start and c == 0 and n == 0), stop=(stop and c == 3 and n == 2))
                        if stop and c == 3:
                            last.then_inc(s_pe[stage], 1)
                    if not (stop and c == 3):
                        last.then_inc(s_pe[stage], 1)

            pe.wait_ge(s_osqrt, 1)
            f = FREED["out_proj"]
            wide_block("out_proj", 0, lambda m: f - 4 + m + 1 if m < 4 else None, 0, start=True)
            wide_block("out_proj", 4, None, 0)
            wide_block("out_proj", 8, None, 0, stop=True)
            feature_sum(1, 0)

            def mlp(layer):
                up, down = f"up{layer}", f"down{layer}"
                o_idx = 1 if layer == 0 else 3
                u0, d0 = FIRST[up], FIRST[down]
                fu, fd = FREED[up] - 8, FREED[down] - 8
                narrow_group(up, 0, 0, lambda j: u0 + j + 1, lambda m: fu + m + 1, opening=o_idx)
                feature_sum(2 * o_idx, 7)
                pe.wait_ge(s_sqrt, 2 * o_idx + 2)
                narrow_group(up, 1, 4, lambda j: u0 + 4 + j + 1, lambda m: fu + 4 + m + 1)
                with pe.Fori(1, 4) as i:
                    for half in range(2):
                        narrow_group(up, None, 4 * half, lambda j: i * 8 + (u0 + 4 * half + j + 1),
                                     lambda m: i * 8 + (fu + 4 * half + m + 1))
                mlo0 = 12 if layer == 0 else 12 + HT + KT
                wide_block(down, 0, lambda m: fd + m + 1, mlo0, start=True)
                with pe.Fori(1, 7) as i:
                    wide_block(down, 0, None, mlo0, i=i)
                wide_block(down, 28, None, mlo0, stop=True)
                feature_sum(2 * o_idx + 1, 0)

            mlp(0)

            p0, fp = FIRST["pw1"], FREED["pw1"] - 8
            narrow_group("pw1", 0, 0, lambda j: p0 + j + 1, lambda m: fp + m + 1, opening=2)
            feature_sum(4, 7)
            pe.wait_ge(s_sqrt, 6)
            for g in range(1, 4):
                narrow_group("pw1", g, 4 * (g % 2), lambda j: p0 + 4 * g + j + 1, lambda m: fp + 4 * g + m + 1)
            pe.wait_ge(s_cv, 1 + KT * (CF_K + 1))
            pe.wait_ge(s_free, FREED["pw2"] - 7)
            nc.tensor.matmul(ps[:, 0, :], ones, acc[:, :], start=True, stop=True).then_inc(s_lnp, 1)
            pe.wait_ge(s_lnadd, KT - 1)
            pe.wait_ge(s_free, FREED["pw2"] - 6)
            nc.tensor.matmul(ps[:, 1, :], ones, acc[:, :], start=True, stop=True).then_inc(s_lnp, 1)
            f2 = FREED["pw2"] - 8
            m2 = 12 + HT
            pe.wait_ge(s_lnroot, 1)
            wide_block("pw2", 0, lambda m: f2 + m + 1, m2, start=True)
            wide_block("pw2", 4, None, m2, stop=True)
            feature_sum(5, 0)
            mlp(1)

        @block.vector
        def _(dve):
            def h_low(m, o_idx, gain):
                dve.wait_ge(s_hhi, KT * o_idx + m + 1)
                nc.vector.scalar_tensor_tensor(h_lo[:, m, :], x[:, m, :], gain, h_hi[:, m, :].bitcast(fp32),
                                               ALU.mult, ALU.subtract).then_inc(s_hlo, 1)

            def add_square(m, norm):
                dve.wait_ge(s_xsq, KT * norm + m + 1)
                if m > 1:
                    dve.wait_ge(s_acc, 7 * norm + m - 1)
                nc.vector.tensor_tensor(acc[:, :], acc[:, :], work[m % 2][:, :], ALU.add).then_inc(s_acc, 1)

            def inverse_rms(root_no):
                dve.wait_ge(s_sqrt, root_no)
                nc.vector.reciprocal(rs[:, :], rs[:, :]).then_inc(s_rs, 1)
                dve.wait_ge(s_rs, root_no)

            dve.wait_ge(s_const, 48)
            for m in range(KT):
                h_low(m, 0, vcol("mix_pre", m))
                if m:
                    add_square(m, 0)
            nc.vector.tensor_copy(mask[:, :], mask_in)
            nc.vector.memset(lr, 1.0).then_inc(s_set, 1)
            dve.wait_ge(s_lr_in, 16)
            gains = vec[:, VEC["mix_pre"]:VEC["mix_pre"] + KT]
            for kk in range(KT):
                last = nc.vector.tensor_scalar(w_lr[:, kk, :], w_lr[:, kk, :], vcol("mix_pre", kk), None, ALU.mult)
            last.then_inc(s_set, 1)

            def evac(stage, g, m, out, bank0, scale=None, done=None):
                dve.wait_ge(s_pe[stage], narrow_bank_done(g, m) if done is None else done)
                if scale is None:
                    return nc.vector.tensor_tensor(out, ps[:, bank0 + m, :], rs[:, :], ALU.mult).then_inc(s_free, 1)
                return nc.vector.scalar_tensor_tensor(out, ps[:, bank0 + m, :], scale, rs[:, :],
                                                      ALU.mult, ALU.mult).then_inc(s_free, 1)

            def halves(t, s):
                return t.rearrange("p (c s) -> p c s", s=s)

            flat = lambda t: t[:, :, :].rearrange("p a n -> p (a n)")
            for n in range(37):
                if n == 4:
                    inverse_rms(1)
                    for m in range(4):
                        evac("in_proj", 0, m, q[:, m, :], 0, scale=float(DK) ** -0.5)
                    dve.wait_ge(s_sqrt, 2)
                    nc.vector.reciprocal(rs_tok[:, :], rs_tok[:, :]).then_inc(s_rs, 1)
                    dve.wait_ge(s_rs, 2)
                if n == 5:
                    dve.wait_ge(s_lrp, 1)
                    dve.wait_ge(s_set, 1)
                    nc.vector.tensor_tensor(lr[0:RANK, :], ps[0:RANK, 4, :], rs[0:RANK, :], ALU.mult).then_inc(s_lr, 1)
                    nc.vector.memset(scores, 0.0).then_inc(s_pred, 1)
                if n == 8:
                    for m in range(4):
                        evac("in_proj", 1, m, k[:, m, :], 0)
                    for t in range(CP):
                        dve.wait_ge(s_sp, 3)
                        nc.vector.scalar_tensor_tensor(g_tok[:, t, :], ps[:, 4 + t, :], 0.0, softp[:, t, :],
                                                       ALU.min, ALU.subtract).then_inc(s_g, 1)
                if n in (12, 16):
                    for m in range(4):
                        c = 512 * (n == 16)
                        dve.wait_ge(s_pe["in_proj"], narrow_bank_done(n // 4 - 1, m))
                        nc.vector.tensor_scalar(v[:, m, c:c + 512], ps[:, m, :], rs_tok[:, m:m + 1], None, ALU.mult).then_inc(s_free, 1)
                if n in (20, 24):
                    for m in range(4):
                        c = m + 4 * (n == 24)
                        evac("in_proj", n // 4 - 1, m, gate[:, c, :], 0)
                if n == 28:
                    for m in range(4):
                        evac("in_proj", 6, m, y_a[:, m, :], 0)
                if n == 32:
                    for m in range(4):
                        evac("in_proj", 7, m, work[m % 2][:, :], 0)
                        dve.wait_ge(s_free, 28 + m + 1)
                        nc.vector.tensor_tensor(sc_p[:, m, :], work[m % 2][:, :], y_a[:, m, :], ALU.mult).then_inc(s_scv, 1)

                if n in (12, 13):
                    half = n - 12
                    dve.wait_ge(s_sc, half + 1)
                    dve.wait_ge(s_pred, 1 + half)
                    dm = mask[:, LEVELS * CHUNK:].rearrange("p (a i) -> p a i", a=1).broadcast_to([P, 8, P])
                    nc.vector.copy_predicated(scores[:, 8 * half:8 * half + 8, :], dm,
                                              ps[:, 4 + 2 * half:6 + 2 * half, :].rearrange("p a (c i) -> p (a c) i", i=P)).then_inc(s_pred, 1)
                lv = n - 13
                if 0 <= lv < LEVELS:
                    s = CHUNK >> lv
                    hf = s // 2
                    nb = HEADS * T // s
                    bb, ee = halves(flat(b), s), halves(e_lv, s)
                    kk_, qq, kl = halves(flat(k), s), halves(flat(q), s), halves(k_lv.rearrange("p a n -> p (a n)"), s)
                    ref = bb[:, :, hf - 1:hf].broadcast_to([P, nb, hf])
                    dve.wait_ge(s_b, 1)
                    if lv:
                        dve.wait_ge(s_qk, 2 * lv)
                    nc.vector.tensor_tensor(ee[:, :, hf:], bb[:, :, hf:], ref, ALU.subtract).then_inc(s_e, 1)
                    nc.vector.tensor_tensor(ee[:, :, :hf], ref, bb[:, :, :hf], ALU.subtract).then_inc(s_e, 1)
                lp = n - 15
                if 0 <= lp < LEVELS:
                    blk = CHUNK >> lp
                    second = blk // 2
                    dve.wait_ge(s_sc, 2 + lp + 1)
                    dve.wait_ge(s_pred, 3 + lp)
                    for bank in range(2):
                        dst = scores[:, 8 * bank:8 * bank + 8, :].rearrange("p c (b s) -> p c b s", s=blk)[:, :, :, second:]
                        src = ps[:, 4 + 2 * (lp % 2) + bank, :].rearrange("p (c b i) -> p c b i", c=8, i=second)
                        mk = mask[:, lp * CHUNK:(lp + 1) * CHUNK].rearrange("p (a b i) -> p a b i", a=1, i=second).broadcast_to([P, 8, CHUNK // second, second])
                        last = nc.vector.copy_predicated(dst, mk, src)
                    last.then_inc(s_pred, 1)
                if 0 <= lv < LEVELS:
                    dve.wait_ge(s_exp, lv + 1)
                    if lv:
                        dve.wait_ge(s_sc, 2 + lv)
                    qv = halves(q_lv, hf)
                    nc.vector.scalar_tensor_tensor(qv, ee[:, :, hf:], 1.0, qq[:, :, hf:], ALU.min, ALU.mult).then_inc(s_qk, 1)
                    nc.vector.scalar_tensor_tensor(kl[:, :, :hf], ee[:, :, :hf], 1.0, kk_[:, :, :hf], ALU.min, ALU.mult).then_inc(s_qk, 1)
                if n == 19:
                    dve.wait_ge(s_exp, LEVELS + 1)
                    nc.vector.scalar_tensor_tensor(flat(q), e_lv, 1.0, flat(q), ALU.min, ALU.mult).then_inc(s_qk, 1)
                    bb = halves(flat(b), CHUNK)
                    last_b = bb[:, :, CHUNK - 1:CHUNK].broadcast_to([P, HEADS * T // CHUNK, CHUNK])
                    dve.wait_ge(s_qk, 2 * LEVELS + 1)
                    nc.vector.tensor_tensor(halves(e_lv, CHUNK), last_b, bb, ALU.subtract).then_inc(s_e, 1)
                if n == 20:
                    dve.wait_ge(s_exp, LEVELS + 2)
                    nc.vector.scalar_tensor_tensor(flat(k), e_lv, 1.0, flat(k), ALU.min, ALU.mult).then_inc(s_qk, 1)
                if 23 <= n < 30:
                    c = n - 23
                    dve.wait_ge(s_u, c + 1)
                    dve.wait_ge(s_el, 1)
                    if c:
                        dve.wait_ge(s_state, HEADS * c)
                    if c >= 3:
                        dve.wait_ge(s_op, (c - 3) // 2 + 1)
                    for hd in range(HEADS):
                        at = hd * DV
                        new = states[:, (c + 1) % RING, at:at + DV]
                        src = ps[:, 6 + hd // 2, at % 512:at % 512 + DV]
                        if c == 0:
                            nc.vector.tensor_copy(new, src).then_inc(s_state, 1)
                        else:
                            nc.vector.scalar_tensor_tensor(new, states[:, c % RING, at:at + DV], e_last[:, hd, c:c + 1], src,
                                                           ALU.mult, ALU.add).then_inc(s_state, 1)
                if n == 32:
                    dve.wait_ge(s_osq, 2)
                    pairs = v[:, :, :].rearrange("p a (h w n) -> p (a h) w n", w=2, n=T)
                    nc.vector.tensor_tensor(b[:, :, :], pairs[:, :, 0, :], pairs[:, :, 1, :], ALU.add).then_inc(s_oadd, 1)
                if n == 33:
                    for m in range(4):
                        wc = lambda tap: vcol("w_sc", tap * 4 + m)
                        dve.wait_ge(s_scv, 4)
                        nc.vector.tensor_scalar(y_a[:, m, :], sc_p[:, m, :], wc(2), None, ALU.mult).then_inc(s_scv, 1)
                        dve.wait_ge(s_scv, 4 + 3 * m + 1)
                        nc.vector.scalar_tensor_tensor(y_a[:, m, 1:], sc_p[:, m, :T - 1], wc(1), y_a[:, m, 1:], ALU.mult, ALU.add).then_inc(s_scv, 1)
                        dve.wait_ge(s_scv, 4 + 3 * m + 2)
                        nc.vector.scalar_tensor_tensor(y_a[:, m, 2:], sc_p[:, m, :T - 2], wc(0), y_a[:, m, 2:], ALU.mult, ALU.add).then_inc(s_scv, 1)
                if n == 34:
                    dve.wait_ge(s_osqrt, 1)
                    nc.vector.reciprocal(q[:, :, :], q[:, :, :]).then_inc(s_ors, 1)
                    dve.wait_ge(s_ors, 1)
                    dve.wait_ge(s_silu, 8)
                    gv = gate[:, :, :].rearrange("p (h w) n -> p h w n", w=2)
                    ov = o[:, :, :].rearrange("p (h w) n -> p h w n", w=2)
                    for w in range(2):
                        nc.vector.tensor_tensor(gv[:, :, w, :], gv[:, :, w, :], q[:, :, :], ALU.mult).then_inc(s_ors, 1)
                    for w in range(2):
                        dve.wait_ge(s_ors, 2 + w)
                        nc.vector.scalar_tensor_tensor(ov[:, :, w, :], ov[:, :, w, :], vcol("gla_g", w), gv[:, :, w, :],
                                                       ALU.mult, ALU.mult).then_inc(s_mid, 1)

            def m_low(src, kk, mhi_no, slot_free=None):
                dve.wait_ge(s_mhi, mhi_no)
                nc.vector.tensor_tensor(m_hl[:, kk % RING, 1, :], src, m_hl[:, kk % RING, 0, :].bitcast(fp32),
                                        ALU.subtract).then_inc(s_mlo, 1)

            for kk in range(3):
                m_low(o[:, kk, :], kk, kk + 1)
            for m in range(4):
                evac("in_proj", 8, m, work[m % 2][:, :], 0)
                dve.wait_ge(s_free, 32 + m + 1)
                dve.wait_ge(s_scv, 4 + 3 * m + 3)
                nc.vector.tensor_tensor(y_a[:, m, :], y_a[:, m, :], work[m % 2][:, :], ALU.mult).then_inc(s_mid, 1)
            for kk in range(3, 8):
                m_low(o[:, kk, :], kk, kk + 1)
            for kk in range(8, 12):
                m_low(y_a[:, kk - 8, :], kk, kk + 1)

            def close(stage, o_idx, gain, gain0, pre, pre0, bias):
                post = 2 * o_idx - 1
                for m in range(KT):
                    dve.wait_ge(s_pe[stage], wide_bank_done(stage, m))
                    nc.vector.tensor_scalar(y[:, m, :], ps[:, m, :], vcol(bias, m) if bias else 0.0, None, ALU.add).then_inc(s_free, 1)
                    if m >= 2:
                        add_square(m - 1, post)
                add_square(KT - 1, post)
                inverse_rms(post + 2)
                if o_idx == 1:
                    dve.wait_ge(s_x_again, 16)
                for m in range(KT):
                    nc.vector.scalar_tensor_tensor(y[:, m, :], y[:, m, :], vcol(gain, gain0 + m), rs[:, :], ALU.mult, ALU.mult).then_inc(s_yn, 1)
                    dve.wait_ge(s_yn, KT * (o_idx - 1) + m + 1)
                    nc.vector.tensor_tensor(x[:, m, :], x[:, m, :], y[:, m, :], ALU.add).then_inc(s_xnew, 1)
                    if pre and m:
                        h_low(m - 1, o_idx, vcol(pre, pre0 + m - 1))
                        if m > 1:
                            add_square(m - 1, 2 * o_idx)
                if pre:
                    h_low(KT - 1, o_idx, vcol(pre, pre0 + KT - 1))
                    add_square(KT - 1, 2 * o_idx)

            def mlp(layer):
                up, down = f"up{layer}", f"down{layer}"
                o_idx = 1 if layer == 0 else 3
                mid_done = 6 if layer == 0 else 6 + HT + KT
                mhi0 = 12 if layer == 0 else 12 + HT + KT
                f_up = FREED[up]

                def evac_group(half, i=None, tile0=0):
                    at = (lambda c, per: c) if i is None else (lambda c, per: i * per + c)
                    g0 = tile0 // 4
                    for m in range(4):
                        dve.wait_ge(s_pe[up], at(narrow_bank_done(g0, m), 14))
                        nc.vector.tensor_tensor(work[m % 2][:, :], ps[:, 4 * half + m, :], rs[:, :], ALU.mult).then_inc(s_free, 1)
                        dve.wait_ge(s_free, at(f_up + tile0 + m + 1, 8))
                        dst = mid[:, tile0 + m, :] if i is None else mid[:, bass.ds(i * 8 + (tile0 + m), 1), :].rearrange("p a n -> p (a n)")
                        nc.vector.scalar_tensor_tensor(dst, work[m % 2][:, :], 0.0, work[m % 2][:, :],
                                                       ALU.max, ALU.mult).then_inc(s_mid, 1)

                inverse_rms(2 * o_idx + 2)
                evac_group(0)
                evac_group(1, tile0=4)
                for kk in range(3):
                    m_low(mid[:, kk, :], kk, mhi0 + kk + 1)
                with dve.Fori(1, 4) as i:
                    evac_group(0, i, 0)
                    evac_group(1, i, 4)
                m_low(mid[:, 3, :], 3, mhi0 + 4)
                with dve.Fori(1, 8) as i:
                    for c in range(4):
                        dve.wait_ge(s_mhi, i * 4 + (mhi0 + c + 1))
                        nc.vector.tensor_tensor(m_hl[:, c, 1, :], mid[:, bass.ds(i * 4 + c, 1), :].rearrange("p a n -> p (a n)"),
                                                m_hl[:, c, 0, :].bitcast(fp32), ALU.subtract).then_inc(s_mlo, 1)
                if layer == 0:
                    close(down, 2, "mlp_post", 0, "mix_pre", KT, None)
                else:
                    close(down, 4, "mlp_post", KT, None, 0, None)

            close("out_proj", 1, "mix_post", 0, "mlp_pre", 0, None)
            mlp(0)

            nc.vector.memset(u[:, :, 0:CF_K - 1], 0.0).then_inc(s_uw, 1)
            inverse_rms(6)
            nc.vector.memset(acc[:, :], 0.0).then_inc(s_cv, 1)
            f = FREED["pw1"]
            for half in range(2):
                for m in range(4):
                    dve.wait_ge(s_pe["pw1"], narrow_bank_done(2 * half, m))
                    nc.vector.tensor_tensor(sg[:, m, :], ps[:, m, :], rs[:, :], ALU.mult).then_inc(s_free, 1)
                for m in range(4):
                    c = 4 * half + m
                    dve.wait_ge(s_pe["pw1"], narrow_bank_done(2 * half + 1, m))
                    nc.vector.tensor_tensor(work[m % 2][:, :], ps[:, 4 + m, :], rs[:, :], ALU.mult).then_inc(s_free, 1)
                    dve.wait_ge(s_free, f + 8 * half + 4 + m + 1)
                    dve.wait_ge(s_sig, c + 1)
                    nc.vector.scalar_tensor_tensor(u[:, c, CF_K - 1:], work[m % 2][:, :], vcol("b_pw1", c), sg[:, m, :],
                                                   ALU.add, ALU.mult).then_inc(s_u1, 1)
                dve.wait_ge(s_uw, 1)
                dve.wait_ge(s_u1, 4 * half + 4)
                per = CF_K + 1
                base = 1 + 4 * per * half
                with dve.Fori(0, 4) as i:
                    tile = dve.snap(i + 4 * half)
                    wcol = dve.snap(i * CF_K + (VEC["w_dw"] + 4 * half * CF_K))
                    bcol = dve.snap(i + (VEC["b_dw"] + 4 * half))
                    ut = lambda tap: u[:, bass.ds(tile, 1), tap:tap + T].rearrange("p a n -> p (a n)")
                    dt_ = d[:, bass.ds(tile, 1), :].rearrange("p a n -> p (a n)")
                    for n in range(CF_K):
                        if n == 0:
                            nc.vector.tensor_scalar(dt_, ut(0), vec[:, bass.ds(wcol, 1)], vec[:, bass.ds(bcol, 1)],
                                                    ALU.mult, ALU.add).then_inc(s_cv, 1)
                        else:
                            dve.wait_ge(s_cv, i * per + (base + n))
                            nc.vector.scalar_tensor_tensor(dt_, ut(n), vec[:, bass.ds(wcol + n, 1)], dt_,
                                                           ALU.mult, ALU.add).then_inc(s_cv, 1)
                    dve.wait_ge(s_cv, i * per + (base + CF_K))
                    nc.vector.tensor_tensor(acc[:, :], acc[:, :], dt_, ALU.add).then_inc(s_cv, 1)

            dve.wait_ge(s_lnp, 1)

            def add_ln_square(m):
                dve.wait_ge(s_lnsq, m + 1)
                if m > 1:
                    dve.wait_ge(s_lnadd, m - 1)
                nc.vector.tensor_tensor(acc[:, :], acc[:, :], work[m % 2][:, :], ALU.add).then_inc(s_lnadd, 1)

            for m in range(KT):
                nc.vector.scalar_tensor_tensor(d[:, m, :], ps[:, 0, :], -1.0 / D, d[:, m, :], ALU.mult, ALU.add).then_inc(s_ln, 1)
                if m > 1:
                    add_ln_square(m - 1)
            add_ln_square(KT - 1)
            dve.wait_ge(s_lnroot, 1)
            nc.vector.reciprocal(rs[:, :], rs[:, :]).then_inc(s_lnrs, 1)
            dve.wait_ge(s_lnrs, 1)
            for m in range(KT):
                nc.vector.tensor_tensor(d[:, m, :], d[:, m, :], rs[:, :], ALU.mult).then_inc(s_z, 1)
                if m >= 3:
                    m_low(act_d[:, m - 3, :], m - 3, 12 + HT + m - 3 + 1)
            for m in range(KT - 3, KT):
                m_low(act_d[:, m, :], m, 12 + HT + m + 1)
            close("pw2", 3, "mix_post", KT, "mlp_pre", KT, "b_pw2")
            mlp(1)


_INS = ["x_t", "w_in", "w_gk2", "b_gk2", "w_out", "w_pw1", "w_pw2", "w_up", "w_down", "vecs", "squares", "masks"]


def _columns(a):
    return np.ascontiguousarray(a.reshape(-1, P).T)


def _shape_constants():
    j, i = np.arange(P)[:, None], np.arange(P)[None, :]
    tri = ((j // CHUNK == i // CHUNK) & (j <= i)) / GATE_NORM
    squares = np.stack([np.ones((P, P)), np.eye(P), tri], axis=1).astype(np.float32)
    levels = []
    for lv in range(LEVELS):
        s = CHUNK >> lv
        n = np.arange(CHUNK)
        row = (n // (s // 2)) * s + s // 2 + n % (s // 2)
        levels.append((j // s == row // s) & (j % s < s // 2))
    return squares, np.concatenate([*levels, j == i], axis=1).astype(np.float32)


def kernel(**inputs):
    import concourse.bacc as bacc
    from concourse.bass_utils import run_bass_kernel_spmd

    a = {n: np.asarray(t) for n, t in inputs.items()}
    squares, masks = _shape_constants()
    dw = a["cf_w_dw"][0].reshape(CF_K, KT, P).transpose(1, 0, 2).reshape(-1)
    parts = [a["norm_mix_pre"], a["norm_mix_post"], a["norm_mlp_pre"], a["norm_mlp_post"], a["cf_b_pw1"], a["cf_b_dw"],
             a["cf_ln_g"], a["cf_ln_b"], a["cf_b_pw2"], a["gla_norm_g"], a["sc_w_conv"], dw]
    cols = [_columns(p) for p in parts]
    cols += [np.full((P, 1), EPS, np.float32), np.zeros((P, 1), np.float32)]
    arrays = {"x_t": a["x"][0].T, "w_in": a["ab_w_in"][0], "w_gk2": a["gla_w_gk2"][0], "b_gk2": a["gla_b_gk2"],
              "w_out": a["ab_w_out"][0], "w_pw1": a["cf_w_pw1"][0], "w_pw2": a["cf_w_pw2"][0],
              "w_up": a["mlp_w1"], "w_down": a["mlp_w2"], "vecs": np.concatenate(cols, axis=1),
              "squares": squares, "masks": masks}
    arrays = {n: np.ascontiguousarray(t) for n, t in arrays.items()}
    nc = bacc.Bacc("TRN2", target_bir_lowering=False, num_devices=1)
    args = [nc.dram_tensor(n, arrays[n].shape, mybir.dt.from_np(arrays[n].dtype), kind="ExternalInput").ap() for n in _INS]
    out_t = nc.dram_tensor("out_t", (D, T), mybir.dt.float32, kind="ExternalOutput").ap()
    build(nc, *args, out_t)
    r = run_bass_kernel_spmd(nc, [arrays], core_ids=[0])
    return np.ascontiguousarray(np.asarray(r.results[0]["out_t"]).T)[None]
```

```python
from contextlib import ExitStack

import concourse.bass as bass
import numpy as np
from concourse import mybir

P = 128
D = 1024
T = 512
KT = D // P
CHUNK = 128
HALF = CHUNK // 2
HEADS = 4
DK = D // 2 // HEADS
DV = D // HEADS
RANK = 16
SCW = D // 2
GATE_NORM = 16.0
CF_K = 31
HID = 4 * D
HT = HID // P
EPS = 1e-6
CP = T // P
LEVELS = 7
PE_TILES = range(4, KT)
PE_TAPS = {4: 15, 5: 15, 6: CF_K, 7: CF_K}
BATCH = 4

VEC_SIZES = [("mix_pre", 2 * KT), ("mix_post", 2 * KT), ("mlp_pre", 2 * KT), ("mlp_post", 2 * KT),
             ("b_pw1", 2 * KT), ("b_dw", KT), ("ln_g", KT), ("ln_b", KT), ("b_pw2", KT),
             ("gla_g", DV // P), ("w_sc", 3 * SCW // P), ("w_dw", CF_K * KT), ("eps", 1), ("zero", 1)]
VEC, _at = {}, 0
for _name, _n in VEC_SIZES:
    VEC[_name] = _at
    _at += _n
NVEC = _at

STAGES = [("in_proj", 36), ("out_proj", 12), ("up0", 32), ("down0", 32), ("pw1", 16), ("pw2", 8),
          ("up1", 32), ("down1", 32)]
FIRST, _at = {}, 0
for _name, _n in STAGES:
    FIRST[_name] = _at
    _at += _n
STEPS = dict(STAGES)
TOTAL_STEPS = _at
RING = 4
AHEAD = 3


def build(nc, x_t, w_in, w_gk2, b_gk2, w_out, w_pw1, w_pw2, w_up, w_down, vecs, squares, masks, out_t):
    fp32, f32r, u8 = mybir.dt.float32, mybir.dt.float32r, mybir.dt.uint8
    ALU, ACT = mybir.AluOpType, mybir.ActivationFunctionType
    ctx = ExitStack()
    with ctx:
        def sb(name, shape, dt=fp32):
            return ctx.enter_context(nc.sbuf_tensor(name, shape, dt))

        def sem(name):
            return ctx.enter_context(nc.semaphore(name))

        x = sb("x", [P, KT, T])
        raw = [sb(f"raw{i}", [P, D]) for i in range(RING)]
        w_hi = [sb(f"w_hi{i}", [P, D], f32r) for i in range(RING)]
        w_lo = [sb(f"w_lo{i}", [P, D], f32r) for i in range(RING)]
        h_hi = sb("h_hi", [P, KT, T], f32r)
        h_lo = sb("h_lo", [P, KT, T], f32r)
        y = sb("y", [P, KT, T])
        vec = sb("vec", [P, NVEC])
        sq_const = sb("sq_const", [P, 3, P])
        mask = sb("mask", [P, LEVELS * HALF + P], u8)
        acc = sb("acc", [P, T])
        work = [sb(f"work{i}", [P, T]) for i in range(2)]
        rs = sb("rs", [P, T])
        r_tok = sb("r_tok", [P, CP])
        ro_tok = sb("ro_tok", [P, HEADS * CP])
        e_last = sb("e_last", [P, HEADS, T // CHUNK])
        w_lr = sb("w_lr", [P, KT, RANK])
        with nc.sbuf_tensor("gate", [P, 2 * HEADS, T], fp32) as gate:
            pass
        m_hl = sb("m_hl", [P, RING, 2, T], f32r)
        with ExitStack() as over:
            def mx(name, shape, dt=fp32):
                return over.enter_context(nc.sbuf_tensor(name, shape, dt))
            y_a = mx("y_a", [P, SCW // P, T])
            o = mx("o", [P, 2 * HEADS, T])
            q = mx("q", [P, HEADS, T])
            k = mx("k", [P, HEADS, T])
            b = mx("b", [P, HEADS, T])
            v = mx("v", [P, CP, HEADS * DV])
        with ExitStack() as over:
            def mx(name, shape, dt=fp32):
                return over.enter_context(nc.sbuf_tensor(name, shape, dt))
            u = mx("u", [P, KT, CF_K - 1 + T])
            d = mx("d", [P, KT, T])
            sg = mx("sg", [P, 2, T])
            diag = mx("diag", [P, 2, 2, BATCH, P], f32r)
            dw_hi = mx("dw_hi", [P, len(PE_TILES) * CF_K], f32r)
            dw_lo = mx("dw_lo", [P, len(PE_TILES) * CF_K])
            with nc.sbuf_tensor("act_d", [P, KT, T], fp32) as act_d:
                pass
            u_hl = mx("u_hl", [P, len(PE_TILES), 2, CF_K - 1 + T], f32r)
        mid = sb("mid", [P, HT, T])

        scores = x[:, 0:4, :].rearrange("p a (c i) -> p (a c) i", i=P)
        q_lv = x[:, 4:6, :].rearrange("p a n -> p (a n)")
        e_lv = o[:, 0:4, :].rearrange("p a n -> p (a n)")
        k_lv = o[:, 4:8, :]
        g_tok = o[:, 0:4, :]
        softp = o[:, 4:8, :]
        kd_tok = b
        sc_p = k
        lr = y[0:RANK + 1, 0, :]
        wgk2 = y[0:RANK + 1, 1, :]
        mask_in = y[:, 2:4, :].rearrange("p a n -> p (a n)")[:, 0:LEVELS * HALF + P]
        states = y[:, :, :].rearrange("p (s a) n -> p s (a n)", s=RING)
        ones = sq_const[:, 0, :]
        ident = sq_const[:, 1, :]
        tri = sq_const[:, 2, :]

        ps = ctx.enter_context(nc.psum_tensor("ps", [P, 8, 512], fp32))

        def vcol(name, c):
            return vec[:, VEC[name] + c:VEC[name] + c + 1]

        eps = vcol("eps", 0)

        s_warm = sem("s_warm")
        s_warm_pe = sem("s_warm_pe")
        s_vec = sem("s_vec")
        s_const = sem("s_const")
        s_lr_in = sem("s_lr_in")
        s_gk_in = sem("s_gk_in")
        s_x = [sem(f"s_x{i}") for i in range(KT)]
        s_x_again = sem("s_x_again")
        s_raw = [sem(f"s_raw{i}") for i in range(RING)]
        s_whi = sem("s_whi")
        s_wlo = sem("s_wlo")
        s_pe = {n: sem(f"s_pe_{n}") for n, _ in STAGES}
        s_free = sem("s_free")
        s_hhi = sem("s_hhi")
        s_hlo = sem("s_hlo")
        s_xsq = sem("s_xsq")
        s_acc = sem("s_acc")
        s_ss = sem("s_ss")
        s_sqrt = sem("s_sqrt")
        s_inv = sem("s_inv")
        s_bc = sem("s_bc")
        s_rs = sem("s_rs")
        s_qn = sem("s_qn")
        s_mid = sem("s_mid")
        s_mhi = sem("s_mhi")
        s_mlo = sem("s_mlo")
        s_yn = sem("s_yn")
        s_xnew = sem("s_xnew")
        s_out = sem("s_out")
        s_set = sem("s_set")
        s_lrp = sem("s_lrp")
        s_lr = sem("s_lr")
        s_gkp = sem("s_gkp")
        s_sp = sem("s_sp")
        s_g = sem("s_g")
        s_bp = sem("s_bp")
        s_b = sem("s_b")
        s_e = sem("s_e")
        s_exp = sem("s_exp")
        s_qk = sem("s_qk")
        s_sc = sem("s_sc")
        s_pred = sem("s_pred")
        s_kdp = sem("s_kdp")
        s_kd = sem("s_kd")
        s_el = sem("s_el")
        s_u = sem("s_u")
        s_state = sem("s_state")
        s_op = sem("s_op")
        s_o = sem("s_o")
        s_osq = sem("s_osq")
        s_oadd = sem("s_oadd")
        s_oss = sem("s_oss")
        s_osqrt = sem("s_osqrt")
        s_ors = sem("s_ors")
        s_obc = sem("s_obc")
        s_silu = sem("s_silu")
        s_og = sem("s_og")
        s_scv = sem("s_scv")
        s_sig = sem("s_sig")
        s_uw = sem("s_uw")
        s_u1 = sem("s_u1")
        s_cv = sem("s_cv")
        s_dwhi = sem("s_dwhi")
        s_dwlo = sem("s_dwlo")
        s_uhi = sem("s_uhi")
        s_ulo = sem("s_ulo")
        s_diagw = sem("s_diagw")
        s_tap = sem("s_tap")
        s_dpe = sem("s_dpe")
        s_dsum = sem("s_dsum")
        s_mean = sem("s_mean")
        s_ln = sem("s_ln")
        s_lnsq = sem("s_lnsq")
        s_lnadd = sem("s_lnadd")
        s_lnss = sem("s_lnss")
        s_lnroot = sem("s_lnroot")
        s_lninv = sem("s_lninv")
        s_lnbc = sem("s_lnbc")
        s_z = sem("s_z")

        block = ctx.enter_context(nc.Block())

        def narrow_step_done(step):
            g, j = divmod(step, 4)
            return 7 * g + (j + 1 if j < 3 else 7)

        def narrow_bank_done(g, m):
            return 7 * g + 3 + m + 1

        def wide_bank_done(stage, m):
            return STEPS[stage] - 2 + m + 1

        FREED = {"in_proj": 0, "out_proj": 36, "up0": 44, "down0": 76, "pw1": 84, "pw2": 100,
                 "up1": 108, "down1": 140}
        WIDE = ("out_proj", "down0", "pw2", "down1")
        GLU_READ = {2: 1, 3: 2, 0: 3, 1: 4}
        BATCHES = [(c, t0, min(BATCH, PE_TAPS[c] - t0)) for c in PE_TILES for t0 in range(0, PE_TAPS[c], BATCH)]
        DONE01, DONE23 = 2 * CF_K, 4 * CF_K
        CONV_DVE = KT * CF_K - sum(PE_TAPS.values())
        ORDER = [n for n, _ in STAGES]

        @block.sync
        def _(sp):
            def narrow_group(w, g0, col, i=None, n=0):
                for j in range(4):
                    step = g0 + j if i is None else None
                    src = w[256 * j:256 * j + 256, bass.ds(col, 512)].rearrange("(a p) n -> p a n", p=P)
                    if i is None:
                        if step >= RING:
                            sp.wait_ge(s_wlo, step - RING + 1)
                    else:
                        sp.wait_ge(s_wlo, i * n + (g0 + j - RING + 1))
                    sp.dma_start(raw[j][:, :].rearrange("p (a n) -> p a n", a=2), src).then_inc(s_raw[j], 16)

            cols = [1536, 2048, 2560, 3072, 3584, 4096, 0, 1024, 512]
            for j in range(4):
                sp.dma_start(raw[j][:, :].rearrange("p (a n) -> p a n", a=2),
                             w_in[256 * j:256 * j + 256, cols[0]:cols[0] + 512].rearrange("(a p) n -> p a n", p=P)).then_inc(s_raw[j], 16)
                for m in (2 * j, 2 * j + 1):
                    sp.dma_start(x[:, m, :], x_t[m * P:(m + 1) * P, :]).then_inc(s_x[m], 16)
            sp.dma_start(sq_const[:, :, :], squares).then_inc(s_const, 16)
            sp.dma_start(mask_in, masks).then_inc(s_const, 16)
            sp.dma_start(w_lr[:, :, :], w_in[:, 4608:4624].rearrange("(a p) n -> p a n", p=P)).then_inc(s_lr_in, 16)
            sp.dma_start(wgk2[0:RANK, :], w_gk2).then_inc(s_gk_in, 16)
            sp.dma_start(wgk2[RANK:RANK + 1, :], b_gk2).then_inc(s_gk_in, 16)
            for g in range(1, 9):
                narrow_group(w_in, 4 * g, cols[g])

            def wide(stage, w, row0, k0, k1):
                base = FIRST[stage]
                with sp.Fori(k0 // 4, k1 // 4) as i:
                    for s in range(4):
                        row = sp.snap(i * 512 + (row0 + s * P))
                        sp.wait_ge(s_wlo, i * 4 + (base + s - RING + 1))
                        sp.dma_start(raw[s][:, :], w[bass.ds(row, P), :]).then_inc(s_raw[s], 16)

            wide("out_proj", w_out, SCW, 0, 8)
            wide("out_proj", w_out, -8 * P, 8, 12)
            sp.wait_ge(s_op, CP)
            sp.dma_start(x[:, :, :], x_t.rearrange("(a p) n -> p a n", p=P)).then_inc(s_x_again, 16)

            def mlp(layer):
                with sp.Fori(0, 8) as i:
                    col = sp.snap(i * 512)
                    narrow_group(w_up[layer], FIRST[f"up{layer}"], col, i, 4)
                wide(f"down{layer}", w_down[layer], 0, 0, HT)

            mlp(0)
            for g in range(4):
                narrow_group(w_pw1, FIRST["pw1"] + 4 * g, 512 * g)
            wide("pw2", w_pw2, 0, 0, KT)
            mlp(1)
            for m in range(KT):
                sp.wait_ge(s_xnew, 3 * KT + m + 1)
                sp.dma_start(out_t[m * P:(m + 1) * P, :], x[:, m, :]).then_inc(s_out, 16)
            sp.wait_ge(s_out, 16 * KT)

        @block.gpsimd
        def _(pool):
            def low_part(s, count):
                pool.wait_ge(s_whi, count)
                nc.gpsimd.tensor_tensor(w_lo[s][:, :], raw[s][:, :], w_hi[s][:, :].bitcast(fp32),
                                        ALU.subtract).then_inc(s_wlo, 1)

            def low_parts(first, last):
                for step in range(first, last):
                    low_part(step % RING, step + 1)

            def low_parts_loop(first, last):
                with pool.Fori(first // RING, last // RING) as i:
                    for s in range(RING):
                        low_part(s, i * RING + (s + 1))

            def u_low(c):
                pool.wait_ge(s_uhi, c - PE_TILES[0] + 1)
                hl = u_hl[:, c - PE_TILES[0], :, :]
                nc.gpsimd.tensor_tensor(hl[:, 1, :], u[:, c, :], hl[:, 0, :].bitcast(fp32), ALU.subtract).then_inc(s_ulo, 1)

            def diagonals(no):
                c, t0, n = BATCHES[no]
                if no >= 2:
                    pool.wait_ge(s_tap, no - 1)
                at = (c - PE_TILES[0]) * CF_K + t0
                for part, w in enumerate((dw_hi[:, :].bitcast(fp32), dw_lo)):
                    nc.gpsimd.tensor_tensor(diag[:, no % 2, part, 0:n, :],
                                            ident.rearrange("p (a i) -> p a i", a=1).broadcast_to([P, n, P]),
                                            w[:, at:at + n].rearrange("p (t a) -> p t a", a=1).broadcast_to([P, n, P]),
                                            ALU.mult).then_inc(s_diagw, 1)

            def d_sum(n):
                if n > 1:
                    pool.wait_ge(s_dsum, n - 1)
                pool.wait_ge(s_cv, DONE01 if n == 1 else DONE23)
                nc.gpsimd.tensor_tensor(acc[:, :], d[:, 0, :] if n == 1 else acc[:, :], d[:, n, :], ALU.add).then_inc(s_dsum, 1)

            pw2 = FIRST["pw2"]
            low_parts_loop(0, pw2 - 8)
            low_parts(pw2 - 8, pw2 - 2)
            pool.wait_ge(s_dwlo, 1)
            diagonals(0)
            diagonals(1)
            low_parts(pw2 - 2, pw2)
            u_low(4)
            u_low(5)
            low_parts(pw2, pw2 + AHEAD)
            for no in range(2, len(BATCHES)):
                diagonals(no)
                if no == 5:
                    u_low(6)
                if no == 9:
                    u_low(7)
                if no == 8:
                    d_sum(1)
                if no == len(BATCHES) - 5:
                    d_sum(2)
                if no == len(BATCHES) - 3:
                    d_sum(3)
                if no == len(BATCHES) - 1:
                    pool.wait_ge(s_dpe, 3)
                    pool.wait_ge(s_dsum, 3)
                    nc.gpsimd.tensor_tensor(acc[:, :], acc[:, :], d[:, 6, :], ALU.add).then_inc(s_dsum, 1)
            for pair in range(3):
                pool.wait_ge(s_lnsq, 2 * pair + 2)
                nc.gpsimd.tensor_tensor(act_d[:, 2 * pair, :], act_d[:, 2 * pair, :], act_d[:, 2 * pair + 1, :],
                                        ALU.add).then_inc(s_lnadd, 1)
            low_parts(pw2 + AHEAD, pw2 + RING)
            low_parts_loop(pw2 + RING, TOTAL_STEPS)

        @block.scalar
        def _(act):
            def w_high(step):
                s = step % RING
                act.wait_ge(s_raw[s], 16 * (step // RING + 1))
                if step >= RING:
                    free = step - RING
                    stage = [n for n in ORDER if FIRST[n] <= free][-1]
                    local = free - FIRST[stage]
                    last = local >= STEPS[stage] - 2
                    done = narrow_step_done(local) if stage not in WIDE else (
                        wide_bank_done(stage, 7) if last else local + 1)
                    act.wait_ge(s_pe[stage], done)
                nc.scalar.activation(w_hi[s][:, :], raw[s][:, :], ACT.Copy).then_inc(s_whi, 1)

            def m_high(src, kk, ready, slot_free):
                if ready is not None:
                    act.wait_ge(*ready)
                if slot_free is not None:
                    act.wait_ge(*slot_free)
                nc.scalar.activation(m_hl[:, kk % RING, 0, :], src, ACT.Copy).then_inc(s_mhi, 1)

            act.dma_start(vec[:, :], vecs).then_inc(s_vec, 16)
            act.wait_ge(s_warm, 1)
            nc.scalar.activation(r_tok[:, :], r_tok[:, :], ACT.Sqrt).then_inc(s_warm, 1)
            act.wait_ge(s_vec, 16)

            def open_tile(m, o_idx, gain, ready):
                act.wait_ge(*ready)
                nc.scalar.activation(h_hi[:, m, :], x[:, m, :], ACT.Copy, scale=gain).then_inc(s_hhi, 1)
                square_tile(m, 2 * o_idx, x)

            def square_tile(m, norm, src, bias=0.0):
                if m >= 3:
                    act.wait_ge(s_acc, 6 * norm + m - 2)
                dst = acc if m == 0 else work[m % 2]
                nc.scalar.activation(dst[:, :], src[:, m, :], ACT.Square, bias=bias).then_inc(s_xsq, 1)

            for m in range(KT):
                if m < 3:
                    w_high(m)
                open_tile(m, 0, vcol("mix_pre", m), (s_x[m], 16))

            def root(norm, sums):
                act.wait_ge(s_ss, norm + 1)
                nc.scalar.activation(r_tok[:, :], sums, ACT.Sqrt, bias=eps, scale=1.0 / D).then_inc(s_sqrt, 1)

            def keep_rs(norm):
                act.wait_ge(s_bc, norm + 1)
                if norm == 0:
                    act.wait_ge(s_warm_pe, 2)
                nc.scalar.activation(rs[:, :], ps[:, 7, :], ACT.Copy).then_inc(s_rs, 1)

            for n in range(36):
                if n == 4:
                    root(0, ps[:, 6, 0:CP])
                w_high(n + AHEAD)
                if n == 5:
                    keep_rs(0)
                if n == 7:
                    act.wait_ge(s_gkp, 1)
                    nc.scalar.activation(softp, ps[:, 4:8, :], ACT.Abs).then_inc(s_sp, 1)
                    act.wait_ge(s_sp, 1)
                    nc.scalar.activation(softp, softp, ACT.Exp, scale=-1.0).then_inc(s_sp, 1)
                    act.wait_ge(s_sp, 2)
                    nc.scalar.activation(softp, softp, ACT.Ln, bias=1.0).then_inc(s_sp, 1)
                if n == 10:
                    act.wait_ge(s_bp, 1)
                    nc.scalar.activation(b[:, :, :], ps[:, 4:8, :], ACT.Copy).then_inc(s_b, 1)
                if 13 <= n < 13 + LEVELS:
                    act.wait_ge(s_e, 2 * (n - 13) + 2)
                    nc.scalar.activation(e_lv, e_lv, ACT.Exp).then_inc(s_exp, 1)
                if n == 20:
                    act.wait_ge(s_qk, 2 * LEVELS)
                    nc.scalar.activation(e_lv, b[:, :, :].rearrange("p a n -> p (a n)"), ACT.Exp).then_inc(s_exp, 1)
                    nc.scalar.activation(e_last[:, :, :], b[:, :, CHUNK - 1::CHUNK], ACT.Exp).then_inc(s_el, 1)
                if n == 21:
                    act.wait_ge(s_e, 2 * LEVELS + 1)
                    nc.scalar.activation(e_lv, e_lv, ACT.Exp).then_inc(s_exp, 1)
                if n == 23:
                    act.wait_ge(s_kdp, 1)
                    nc.scalar.activation(kd_tok[:, :, :], ps[:, 4:8, :], ACT.Copy).then_inc(s_kd, 1)
                if n in (22, 25):
                    for t in range(4):
                        c = t + (4 if n == 25 else 0)
                        act.wait_ge(s_free, 16 + c + 1)
                        nc.scalar.activation(gate[:, c, :], gate[:, c, :], ACT.Silu).then_inc(s_silu, 1)
                if n in (25, 27, 29, 31):
                    c = (n - 25) // 2
                    act.wait_ge(s_op, c + 1)
                    nc.scalar.activation(o[:, :, c * P:(c + 1) * P],
                                         ps[:, 4:6, :].rearrange("p a (c n) -> p (a c) n", n=P), ACT.Copy).then_inc(s_o, 1)
                    act.wait_ge(s_o, c + 1)
                    nc.scalar.activation(v[:, c, :].rearrange("p (a n) -> p a n", n=P), o[:, :, c * P:(c + 1) * P],
                                         ACT.Square).then_inc(s_osq, 1)
                if n == 32:
                    act.wait_ge(s_oss, 1)
                    nc.scalar.activation(ro_tok[:, :], ps[:, 4, 0:HEADS * CP], ACT.Sqrt, bias=eps, scale=1.0 / DV).then_inc(s_osqrt, 1)

            def wide_stage(stage, tiles, mid0, ready, first=0):
                base = FIRST[stage]
                for kk in range(first, 3):
                    m_high(tiles(kk), mid0 + kk, ready(kk), None)
                n = STEPS[stage]
                for kk in range(n):
                    if kk < n - 1:
                        w_high(base + kk + AHEAD)
                    if kk + 3 < n:
                        m_high(tiles(kk + 3), mid0 + kk + 3, ready(kk + 3), (s_pe[stage], kk) if kk else None)

            def close(stage, o_idx, pre):
                post = 2 * o_idx - 1
                for m in range(KT):
                    act.wait_ge(s_pe[stage], wide_bank_done(stage, m))
                    square_tile(m, post, ps, vcol("b_pw2", m) if stage == "pw2" else 0.0)
                root(post, ps[:, 0:CP, 0])
                if pre:
                    after = FIRST[stage] + STEPS[stage]
                    w_high(after + AHEAD - 1)
                    for m in range(KT):
                        if m == 2:
                            w_high(after + AHEAD)
                        open_tile(m, o_idx, vcol(pre[0], pre[1] + m), (s_xnew, KT * (o_idx - 1) + m + 1))

            out_tiles = [o[:, c, :] for c in range(8)] + [y_a[:, c, :] for c in range(4)]
            wide_stage("out_proj", lambda kk: out_tiles[kk], 0,
                       lambda kk: (s_mid, 1 if kk < 2 else 2) if kk < 8 else (s_mid, 2 + kk - 7))
            close("out_proj", 1, ("mlp_pre", 0))

            def mlp(layer):
                up, down = f"up{layer}", f"down{layer}"
                o_idx = 1 if layer == 0 else 3
                mid_done = 6 if layer == 0 else 6 + HT + KT
                mhi0 = 12 if layer == 0 else 12 + HT + KT
                u0, d0 = FIRST[up], FIRST[down]
                for n in range(8):
                    if n == 4:
                        root(2 * o_idx, ps[:, 7, 0:CP])
                    if n:
                        w_high(u0 + n + AHEAD)
                    if n == 4:
                        keep_rs(2 * o_idx)
                for kk in range(3):
                    m_high(mid[:, kk, :], kk, (s_mid, mid_done + kk + 1), None)
                with act.Fori(1, 4) as i:
                    for n in range(8):
                        s = (n + AHEAD) % RING
                        act.wait_ge(s_raw[s], i * 32 + 16 * ((u0 + n + AHEAD) // RING + 1))
                        if n == 0:
                            act.wait_ge(s_pe[up], i * 14)
                        else:
                            act.wait_ge(s_pe[up], i * 14 + narrow_step_done(n - 1))
                        nc.scalar.activation(w_hi[s][:, :], raw[s][:, :], ACT.Copy).then_inc(s_whi, 1)
                for kk in range(4):
                    w_high(d0 + kk + AHEAD)
                    m_high(mid[:, kk + 3, :], kk + 3, (s_mid, mid_done + kk + 4), (s_pe[down], kk) if kk else None)
                with act.Fori(1, 7) as i:
                    for c in range(4):
                        s = (c + AHEAD) % RING
                        act.wait_ge(s_raw[s], i * 16 + 16 * ((d0 + c + AHEAD) // RING + 1))
                        act.wait_ge(s_pe[down], i * 4 + c)
                        nc.scalar.activation(w_hi[s][:, :], raw[s][:, :], ACT.Copy).then_inc(s_whi, 1)
                        act.wait_ge(s_mid, i * 4 + (mid_done + c + 4))
                        nc.scalar.activation(m_hl[:, s, 0, :], mid[:, bass.ds(i * 4 + (c + 3), 1), :].rearrange("p a n -> p (a n)"),
                                             ACT.Copy).then_inc(s_mhi, 1)
                for kk in range(28, 32):
                    if d0 + kk + AHEAD < TOTAL_STEPS and kk < HT - 1:
                        w_high(d0 + kk + AHEAD)
                    if kk + 3 < HT:
                        m_high(mid[:, kk + 3, :], kk + 3, (s_mid, mid_done + kk + 4), (s_pe[down], kk))
                close(down, o_idx + 1, ("mix_pre", KT) if layer == 0 else None)

            mlp(0)

            def sigmoids(g):
                for t in range(2):
                    act.wait_ge(s_free, FREED["pw1"] + 4 * g + t + 1)
                    nc.scalar.activation(sg[:, t, :], sg[:, t, :], ACT.Sigmoid, bias=vcol("b_pw1", KT + 2 * g + t)).then_inc(s_sig, 1)

            def u_high(c):
                act.wait_ge(s_uw, 1)
                act.wait_ge(s_u1, c + 1)
                nc.scalar.activation(u_hl[:, c - PE_TILES[0], 0, :], u[:, c, :], ACT.Copy).then_inc(s_uhi, 1)

            p0 = FIRST["pw1"]
            for n in range(16):
                if n == 4:
                    root(4, ps[:, 7, 0:CP])
                if n:
                    w_high(p0 + n + AHEAD)
                if n == 4:
                    keep_rs(4)
                if n == 2:
                    nc.scalar.activation(dw_hi[:, :], vec[:, VEC["w_dw"] + PE_TILES[0] * CF_K:VEC["w_dw"] + KT * CF_K],
                                         ACT.Copy).then_inc(s_dwhi, 1)
                if n in (5, 9, 13):
                    sigmoids(n // 4 - 1)
                if n == 13:
                    u_high(4)
                    u_high(5)
            sigmoids(3)
            u_high(6)
            u_high(7)
            for c in PE_TILES:
                act.wait_ge(s_tap, sum(1 for no in BATCHES if no[0] <= c))
                nc.scalar.activation(d[:, c, :], ps[:, c - PE_TILES[0], :], ACT.Identity, bias=vcol("b_dw", c)).then_inc(s_dpe, 1)
            for m in range(KT):
                act.wait_ge(s_ln, m + 1)
                nc.scalar.activation(act_d[:, m, :], d[:, m, :], ACT.Square).then_inc(s_lnsq, 1)
            act.wait_ge(s_lnss, 1)
            nc.scalar.activation(r_tok[:, :], ps[:, 0:CP, 0], ACT.Sqrt, bias=eps, scale=1.0 / D).then_inc(s_lnroot, 1)

            def silu_tile(m):
                act.wait_ge(s_z, m + 1)
                nc.scalar.activation(act_d[:, m, :], d[:, m, :], ACT.Silu, bias=vcol("ln_b", m),
                                     scale=vcol("ln_g", m)).then_inc(s_mid, 1)

            mid0 = 6 + HT
            for m in range(3):
                silu_tile(m)
                m_high(act_d[:, m, :], m, (s_mid, mid0 + m + 1), None)
            q0 = FIRST["pw2"]
            for kk in range(KT):
                if kk < KT - 1:
                    w_high(q0 + kk + AHEAD)
                if kk + 3 < KT:
                    silu_tile(kk + 3)
                    m_high(act_d[:, kk + 3, :], kk + 3, (s_mid, mid0 + kk + 4), (s_pe["pw2"], kk) if kk else None)
            close("pw2", 3, ("mlp_pre", KT))
            mlp(1)

        @block.tensor
        def _(pe):
            PASSES = ((0, 0), (1, 0), (0, 1))
            WARM = (0, 3, 12, 14, 2, 3, 14, 16)

            def h(kk, part):
                return (h_hi, h_lo)[part][:, kk, :]

            def wt(s, part, c, n=P):
                return (w_hi, w_lo)[part][s][:, c:c + n]

            def narrow_group(stage, g, bank0, step_of, bank_free, tokens_out=False, after=None, opening=None, norm=None):
                def product(j, kk, m, passes):
                    c = (kk % 2) * 512
                    for n in passes:
                        wp, hp = PASSES[n]
                        if tokens_out:
                            lhs, rhs = h(kk, hp)[:, m * P:(m + 1) * P], wt(j, wp, c, 512)
                        else:
                            lhs, rhs = wt(j, wp, c + m * P), h(kk, hp)
                        last = nc.tensor.matmul(ps[:, bank0 + m, :], lhs, rhs,
                                                start=(kk == 0 and n == 0), stop=(kk == KT - 1 and n == 2))
                    return last

                for j in range(4):
                    if opening is None:
                        pe.wait_ge(s_wlo, step_of(j))
                    pair = (2 * j, 2 * j + 1)
                    if norm is not None and j == 0:
                        for kk in pair:
                            for m in range(3):
                                if kk == 0 and bank_free(m) is not None:
                                    pe.wait_ge(s_free, bank_free(m))
                                product(j, kk, m, (0, 1, 2))
                            if kk == 0:
                                broadcast(norm)
                        pe.wait_ge(s_rs, norm // 2 + 1)
                        pe.wait_ge(s_free, bank_free(3))
                        for kk in pair:
                            last = product(j, kk, 3, (0, 1, 2))
                        last.then_inc(s_pe[stage], 1)
                        continue
                    for kk in pair:
                        for part in (((0,), (1,), (2,)) if opening is not None else ((0, 1, 2),)):
                            if opening is not None:
                                if part[0] == 0:
                                    pe.wait_ge(s_whi, step_of(j))
                                    pe.wait_ge(s_hhi, KT * opening + kk + 1)
                                elif part[0] == 1:
                                    pe.wait_ge(s_wlo, step_of(j))
                                else:
                                    pe.wait_ge(s_hlo, KT * opening + kk + 1)
                            for m in range(4):
                                if kk == 0 and part[0] == 0 and bank_free(m) is not None:
                                    pe.wait_ge(s_free, bank_free(m))
                                last = product(j, kk, m, part)
                                if kk == KT - 1 and part[-1] == 2:
                                    last.then_inc(s_pe[stage], 1)
                    if j < 3:
                        last.then_inc(s_pe[stage], 1)
                    if after is not None:
                        after(4 * g + j)

            def keep_warm(n, bank=0):
                for _ in range(n):
                    nc.tensor.matmul(ps[:, bank, 0:P], ones, ident, start=True, stop=True)

            def token_sums(norm, bank):
                pe.wait_ge(s_acc, 6 * (norm + 1))
                pe.wait_ge(s_xsq, KT * (norm + 1))
                for t in range(CP):
                    nc.tensor.matmul(ps[:, bank, t:t + 1], acc[:, t * P:(t + 1) * P], ones[:, 0:1], start=True, stop=False)
                    last = nc.tensor.matmul(ps[:, bank, t:t + 1], work[1][:, t * P:(t + 1) * P], ones[:, 0:1], start=False, stop=True)
                last.then_inc(s_ss, 1)

            def to_all_partitions(bank, per_token, col):
                for t in range(CP):
                    last = nc.tensor.matmul(ps[:, bank, t * P:(t + 1) * P], per_token[:, col + t:col + t + 1].broadcast_to([P, P]), ident,
                                            start=True, stop=True)
                return last

            def broadcast(norm):
                pe.wait_ge(s_inv, norm + 1)
                to_all_partitions(7, r_tok, 0).then_inc(s_bc, 1)

            def column_sums(tile, start, stop, m=None):
                for t in range(CP):
                    last = nc.tensor.matmul(ps[:, t, 0:1], tile[:, t * P:(t + 1) * P], ones[:, 0:1], start=start, stop=stop)
                return last

            def post_norm(stage, norm):
                pe.wait_ge(s_free, FREED[stage] + 5)
                pe.wait_ge(s_acc, 6 * (norm + 1))
                column_sums(acc, True, False)
                keep_warm(WARM[0], 4)
                pe.wait_ge(s_xsq, KT * (norm + 1))
                column_sums(work[1], False, True).then_inc(s_ss, 1)
                keep_warm(WARM[1], 4)
                pe.wait_ge(s_free, FREED[stage] + KT)
                broadcast(norm)
                if norm < 7:
                    keep_warm(WARM[2], 4)

            def gla(n):
                if n == 3:
                    pe.wait_ge(s_const, 32)
                    token_sums(0, 6)
                if n == 4:
                    broadcast(0)
                    pe.wait_ge(s_set, 2)
                    for kk in range(KT):
                        last = nc.tensor.matmul(ps[0:RANK, 4, :], w_lr[:, kk, :], x[:, kk, :], start=(kk == 0), stop=(kk == KT - 1))
                    last.then_inc(s_lrp, 1)
                if n == 6:
                    pe.wait_ge(s_lr, 1)
                    pe.wait_ge(s_gk_in, 32)
                    pe.wait_ge(s_rs, 1)
                    for t in range(CP):
                        last = nc.tensor.matmul(ps[:, 4 + t, :], lr[:, t * P:(t + 1) * P], wgk2, start=True, stop=True)
                    last.then_inc(s_gkp, 1)
                if n == 9:
                    pe.wait_ge(s_g, CP)
                    for hd in range(HEADS):
                        for t in range(CP):
                            last = nc.tensor.matmul(ps[:, 4 + hd, t * P:(t + 1) * P], g_tok[:, t, hd * P:(hd + 1) * P], tri,
                                                    start=True, stop=True)
                    last.then_inc(s_bp, 1)
                if n in (11, 12):
                    half = n - 11
                    pe.wait_ge(s_b, 1)
                    pe.wait_ge(s_free, 8)
                    pe.wait_ge(s_qn, HEADS)
                    for hd in (2 * half, 2 * half + 1):
                        for c in range(CP):
                            last = nc.tensor.matmul(ps[:, 4 + hd, c * P:(c + 1) * P], k[:, hd, c * P:(c + 1) * P],
                                                    q[:, hd, c * P:(c + 1) * P], start=True, stop=True)
                    last.then_inc(s_sc, 1)
                if 14 <= n < 14 + LEVELS:
                    lv = n - 14
                    pe.wait_ge(s_qk, 2 * lv + 2)
                    pe.wait_ge(s_pred, lv + 2)
                    for hd in range(HEADS):
                        for c in range(CP):
                            at = (hd * CP + c) * HALF
                            last = nc.tensor.matmul(ps[:, 4 + 2 * (lv % 2) + hd // 2, at % 512:at % 512 + HALF],
                                                    k_lv[:, hd, c * P:(c + 1) * P], q_lv[:, at:at + HALF],
                                                    start=True, stop=True)
                    last.then_inc(s_sc, 1)
                if n == 22:
                    pe.wait_ge(s_qk, 2 * LEVELS + 2)
                    pe.wait_ge(s_pred, LEVELS + 3)
                    for c in range(CP):
                        for hd in range(HEADS):
                            last = nc.tensor.transpose(ps[:, 4 + c, hd * P:(hd + 1) * P], k[:, hd, c * P:(c + 1) * P], ident)
                    last.then_inc(s_kdp, 1)

                if n in (23, 25, 27):
                    c = (n - 23) // 2
                    if c == 0:
                        pe.wait_ge(s_kd, 1)
                        pe.wait_ge(s_free, 16)
                    else:
                        pe.wait_ge(s_state, HEADS * c)
                    for hd in range(HEADS):
                        at = hd * DV
                        last = nc.tensor.matmul(ps[:, 6 + hd // 2, at % 512:at % 512 + DV], kd_tok[:, c, hd * P:(hd + 1) * P],
                                                v[:, c, at:at + DV], start=True, stop=True)
                    last.then_inc(s_u, 1)
                if n in (24, 26, 28, 30):
                    c = (n - 24) // 2
                    if c:
                        pe.wait_ge(s_o, c)
                        pe.wait_ge(s_state, HEADS * c)
                    for hd in range(HEADS):
                        for w in range(2):
                            at = (2 * hd + w) * P
                            bank, at = 4 + at // 512, at % 512
                            col = hd * DV + w * P
                            last = nc.tensor.matmul(ps[:, bank, at:at + P], v[:, c, col:col + P], scores[:, hd * CP + c, :],
                                                    start=True, stop=(c == 0))
                            if c:
                                last = nc.tensor.matmul(ps[:, bank, at:at + P], states[:, c, col:col + P],
                                                        q[:, hd, c * P:(c + 1) * P], start=False, stop=True)
                    last.then_inc(s_op, 1)
                if n == 31:
                    pe.wait_ge(s_oadd, CP)
                    for hd in range(HEADS):
                        for c in range(CP):
                            last = nc.tensor.matmul(ps[:, 4, hd * CP + c:hd * CP + c + 1], v[:, c, hd * DV:hd * DV + P],
                                                    ones[:, 0:1], start=True, stop=True)
                    last.then_inc(s_oss, 1)
                if n == 33:
                    pe.wait_ge(s_ors, 1)
                    for hd in range(HEADS):
                        last = to_all_partitions(4 + hd, ro_tok, hd * CP)
                    last.then_inc(s_obc, 1)

            pe.wait_ge(s_warm_pe, 1)
            for _ in range(WARM[7]):
                last = nc.tensor.matmul(ps[:, 0, 0:P], rs[:, 0:P], rs[:, P:2 * P], start=True, stop=True)
            last.then_inc(s_warm_pe, 1)
            for g in range(9):
                narrow_group("in_proj", g, 0, lambda j: 4 * g + j + 1, lambda m: 4 * (g - 1) + m + 1 if g else None,
                             tokens_out=g in (2, 3), after=gla, opening=0 if g == 0 else None)

            def wide_block(stage, k0, banks_free, mlo0, i=None, start=False, stop=False, bank7=None):
                base = FIRST[stage]

                def product(c, m):
                    for n, (wp, hp) in enumerate(PASSES):
                        last = nc.tensor.matmul(ps[:, m, :], wt(c, wp, m * P), m_hl[:, c, hp, :],
                                                start=(start and c == 0 and n == 0), stop=(stop and c == 3 and n == 2))
                    return last

                for c in range(4):
                    if i is None:
                        pe.wait_ge(s_wlo, base + k0 + c + 1)
                        pe.wait_ge(s_mlo, mlo0 + k0 + c + 1)
                    else:
                        pe.wait_ge(s_wlo, i * 4 + (base + c + 1))
                        pe.wait_ge(s_mlo, i * 4 + (mlo0 + c + 1))
                    if stop and c == 2:
                        continue
                    for m in range(8):
                        if start and c == 0 and banks_free(m) is not None:
                            pe.wait_ge(s_free, banks_free(m))
                        if bank7 is not None and c == 0 and m == 7:
                            pe.wait_ge(*bank7)
                        if stop and c == 3:
                            product(2, m)
                            product(3, m).then_inc(s_pe[stage], 1)
                        else:
                            last = product(c, m)
                    if not (stop and c == 3):
                        last.then_inc(s_pe[stage], 1)

            pe.wait_ge(s_mid, 2)
            f = FREED["out_proj"]
            wide_block("out_proj", 0, lambda m: f - 4 + m + 1 if m < 4 else None, 0, start=True)
            wide_block("out_proj", 4, None, 0)
            wide_block("out_proj", 8, None, 0, stop=True)
            post_norm("out_proj", 1)

            def mlp(layer):
                up, down = f"up{layer}", f"down{layer}"
                o_idx = 1 if layer == 0 else 3
                u0, d0 = FIRST[up], FIRST[down]
                fu, fd = FREED[up] - 8, FREED[down] - 8
                narrow_group(up, 0, 0, lambda j: u0 + j + 1, lambda m: fu + m + 1, opening=o_idx)
                token_sums(2 * o_idx, 7)
                narrow_group(up, 1, 4, lambda j: u0 + 4 + j + 1, lambda m: fu + 4 + m + 1, norm=2 * o_idx)
                with pe.Fori(1, 4) as i:
                    for half in range(2):
                        narrow_group(up, None, 4 * half, lambda j: i * 8 + (u0 + 4 * half + j + 1),
                                     lambda m: i * 8 + (fu + 4 * half + m + 1))
                mlo0 = 12 if layer == 0 else 12 + HT + KT
                wide_block(down, 0, lambda m: fd + m + 1, mlo0, start=True)
                with pe.Fori(1, 7) as i:
                    wide_block(down, 0, None, mlo0, i=i)
                wide_block(down, 28, None, mlo0, stop=True)
                post_norm(down, 2 * o_idx + 1)

            mlp(0)

            p0, fp = FIRST["pw1"], FREED["pw1"] - 8
            narrow_group("pw1", 0, 0, lambda j: p0 + j + 1, lambda m: fp + m + 1, opening=2)
            token_sums(4, 7)
            narrow_group("pw1", 1, 4, lambda j: p0 + 4 + j + 1, lambda m: fp + 4 + m + 1, norm=4)
            for g in (2, 3):
                narrow_group("pw1", g, 4 * (g % 2), lambda j: p0 + 4 * g + j + 1,
                             lambda m: FREED["pw1"] + 4 * (g - 2) + GLU_READ[m])

            pe.wait_ge(s_free, FREED["pw1"] + 12)
            for no, (c, t0, n) in enumerate(BATCHES):
                i = c - PE_TILES[0]
                if t0 == 0:
                    pe.wait_ge(s_ulo, i + 1)
                for j, (wp, up_) in enumerate(PASSES):
                    if j < 2:
                        pe.wait_ge(s_diagw, 2 * no + j + 1)
                    for t in range(n):
                        last = nc.tensor.matmul(ps[:, i, :], diag[:, no % 2, wp, t, :], u_hl[:, i, up_, t0 + t:t0 + t + T],
                                                start=(t0 + t == 0 and j == 0), stop=(t0 + t == PE_TAPS[c] - 1 and j == 2))
                last.then_inc(s_tap, 1)

            pe.wait_ge(s_free, FREED["pw2"])
            pe.wait_ge(s_dsum, 4)
            nc.tensor.matmul(ps[:, 4, :], ones, acc[:, :], start=True, stop=False)
            pe.wait_ge(s_cv, CONV_DVE)
            nc.tensor.matmul(ps[:, 4, :], ones, d[:, 4, :], start=False, stop=False)
            nc.tensor.matmul(ps[:, 4, :], ones, d[:, 5, :], start=False, stop=False)
            pe.wait_ge(s_dpe, 4)
            nc.tensor.matmul(ps[:, 4, :], ones, d[:, 7, :], start=False, stop=True).then_inc(s_mean, 1)
            keep_warm(WARM[3], 5)
            for n, (src, ready) in enumerate(((0, (s_lnadd, 1)), (2, (s_lnadd, 2)), (6, (s_lnsq, 7)),
                                              (4, (s_lnadd, 3)), (7, (s_lnsq, 8)))):
                keep_warm(WARM[4] if n else 0, 5)
                pe.wait_ge(*ready)
                last = column_sums(act_d[:, src, :], n == 0, n == 4)
            last.then_inc(s_lnss, 1)
            keep_warm(WARM[5], 5)
            pe.wait_ge(s_lninv, 1)
            to_all_partitions(7, r_tok, 0).then_inc(s_lnbc, 1)
            keep_warm(WARM[6], 5)
            f2 = FREED["pw2"] - 8
            m2 = 12 + HT
            wide_block("pw2", 0, lambda m: f2 + m + 1, m2, start=True, bank7=(s_z, KT))
            wide_block("pw2", 4, None, m2, stop=True)
            post_norm("pw2", 5)
            mlp(1)

        @block.vector
        def _(dve):
            def h_low(m, o_idx, gain):
                dve.wait_ge(s_hhi, KT * o_idx + m + 1)
                nc.vector.scalar_tensor_tensor(h_lo[:, m, :], x[:, m, :], gain, h_hi[:, m, :].bitcast(fp32),
                                               ALU.mult, ALU.subtract).then_inc(s_hlo, 1)

            def add_square(m, norm):
                dve.wait_ge(s_xsq, KT * norm + m + 1)
                if m > 1:
                    dve.wait_ge(s_acc, 6 * norm + m - 1)
                nc.vector.tensor_tensor(acc[:, :], acc[:, :], work[m % 2][:, :], ALU.add).then_inc(s_acc, 1)

            def inverse_rms(norm):
                dve.wait_ge(s_sqrt, norm + 1)
                nc.vector.reciprocal(r_tok[:, :], r_tok[:, :]).then_inc(s_inv, 1)

            nc.vector.memset(r_tok[:, :], 0.0).then_inc(s_warm, 1)
            nc.vector.memset(rs[:, :], 0.0).then_inc(s_warm_pe, 1)
            dve.wait_ge(s_vec, 16)
            for m in range(KT):
                h_low(m, 0, vcol("mix_pre", m))
                if 0 < m < KT - 1:
                    add_square(m, 0)
            dve.wait_ge(s_const, 32)
            nc.vector.tensor_copy(mask[:, :], mask_in)
            nc.vector.memset(lr, 1.0).then_inc(s_set, 1)
            dve.wait_ge(s_lr_in, 16)
            for kk in range(KT):
                last = nc.vector.tensor_scalar(w_lr[:, kk, :], w_lr[:, kk, :], vcol("mix_pre", kk), None, ALU.mult)
            last.then_inc(s_set, 1)

            def evac(stage, g, m, out, bank0):
                dve.wait_ge(s_pe[stage], narrow_bank_done(g, m))
                return nc.vector.tensor_tensor(out, ps[:, bank0 + m, :], rs[:, :], ALU.mult).then_inc(s_free, 1)

            def halves(t, s):
                return t.rearrange("p (c s) -> p c s", s=s)

            flat = lambda t: t[:, :, :].rearrange("p a n -> p (a n)")

            def at_level(lv):
                s = CHUNK >> lv
                return s, s // 2, halves(flat(b), s), halves(flat(k), s), halves(flat(q), s), halves(k_lv.rearrange("p a n -> p (a n)"), s)

            for n in range(37):
                if n == 4:
                    for m in range(4):
                        dve.wait_ge(s_pe["in_proj"], narrow_bank_done(0, m))
                        nc.vector.tensor_copy(q[:, m, :], ps[:, m, :]).then_inc(s_free, 1)
                    inverse_rms(0)
                if n == 5:
                    dve.wait_ge(s_rs, 1)
                    dve.wait_ge(s_free, HEADS)
                    for m in range(4):
                        nc.vector.scalar_tensor_tensor(q[:, m, :], q[:, m, :], float(DK) ** -0.5, rs[:, :],
                                                       ALU.mult, ALU.mult).then_inc(s_qn, 1)
                    dve.wait_ge(s_lrp, 1)
                    dve.wait_ge(s_set, 1)
                    nc.vector.tensor_tensor(lr[0:RANK, :], ps[0:RANK, 4, :], rs[0:RANK, :], ALU.mult).then_inc(s_lr, 1)
                    nc.vector.memset(scores, 0.0).then_inc(s_pred, 1)
                if n == 8:
                    for m in range(4):
                        evac("in_proj", 1, m, k[:, m, :], 0)
                    for t in range(CP):
                        dve.wait_ge(s_sp, 3)
                        nc.vector.scalar_tensor_tensor(g_tok[:, t, :], ps[:, 4 + t, :], 0.0, softp[:, t, :],
                                                       ALU.min, ALU.subtract).then_inc(s_g, 1)
                if n in (12, 16):
                    for m in range(4):
                        c = 512 * (n == 16)
                        dve.wait_ge(s_pe["in_proj"], narrow_bank_done(n // 4 - 1, m))
                        nc.vector.tensor_scalar(v[:, m, c:c + 512], ps[:, m, :], r_tok[:, m:m + 1], None, ALU.mult).then_inc(s_free, 1)
                if n in (20, 24):
                    for m in range(4):
                        c = m + 4 * (n == 24)
                        evac("in_proj", n // 4 - 1, m, gate[:, c, :], 0)
                if n == 28:
                    for m in range(4):
                        evac("in_proj", 6, m, y_a[:, m, :], 0)
                if n == 32:
                    for m in range(4):
                        evac("in_proj", 7, m, sc_p[:, m, :], 0)
                if n == 33:
                    dve.wait_ge(s_free, 32)
                    nc.vector.tensor_tensor(sc_p[:, :, :], sc_p[:, :, :], y_a[:, :, :], ALU.mult).then_inc(s_scv, 1)

                if n in (12, 13):
                    half = n - 12
                    dve.wait_ge(s_sc, half + 1)
                    dve.wait_ge(s_pred, 1 + half)
                    dm = mask[:, LEVELS * HALF:].rearrange("p (a i) -> p a i", a=1).broadcast_to([P, 8, P])
                    nc.vector.copy_predicated(scores[:, 8 * half:8 * half + 8, :], dm,
                                              ps[:, 4 + 2 * half:6 + 2 * half, :].rearrange("p a (c i) -> p (a c) i", i=P)).then_inc(s_pred, 1)
                lv = n - 14
                if 0 <= lv < LEVELS:
                    s, hf, _, kk_, qq, kl = at_level(lv)
                    ee = halves(e_lv, s)
                    dve.wait_ge(s_exp, lv + 1)
                    if lv:
                        dve.wait_ge(s_sc, 2 + lv)
                    nc.vector.scalar_tensor_tensor(halves(q_lv, hf), ee[:, :, hf:], 1.0, qq[:, :, hf:], ALU.min, ALU.mult).then_inc(s_qk, 1)
                    nc.vector.scalar_tensor_tensor(kl[:, :, :hf], ee[:, :, :hf], 1.0, kk_[:, :, :hf], ALU.min, ALU.mult).then_inc(s_qk, 1)
                lp = n - 15
                if 0 <= lp < LEVELS:
                    blk = CHUNK >> lp
                    second = blk // 2
                    dve.wait_ge(s_sc, 2 + lp + 1)
                    dve.wait_ge(s_pred, 3 + lp)
                    for bank in range(2):
                        dst = scores[:, 8 * bank:8 * bank + 8, :].rearrange("p c (b s) -> p c b s", s=blk)[:, :, :, second:]
                        src = ps[:, 4 + 2 * (lp % 2) + bank, :].rearrange("p (c b i) -> p c b i", c=8, i=second)
                        mk = mask[:, lp * HALF:(lp + 1) * HALF].rearrange("p (a b i) -> p a b i", a=1, i=second).broadcast_to([P, 8, HALF // second, second])
                        last = nc.vector.copy_predicated(dst, mk, src)
                    last.then_inc(s_pred, 1)
                lv = n - 13
                if 0 <= lv < LEVELS:
                    s, hf, bb, _, _, _ = at_level(lv)
                    ee = halves(e_lv, s)
                    ref = bb[:, :, hf - 1:hf].broadcast_to([P, HEADS * T // s, hf])
                    dve.wait_ge(s_b, 1)
                    if lv:
                        dve.wait_ge(s_qk, 2 * lv)
                    nc.vector.tensor_tensor(ee[:, :, hf:], bb[:, :, hf:], ref, ALU.subtract).then_inc(s_e, 1)
                    nc.vector.tensor_tensor(ee[:, :, :hf], ref, bb[:, :, :hf], ALU.subtract).then_inc(s_e, 1)
                if n == 21:
                    dve.wait_ge(s_exp, LEVELS + 1)
                    nc.vector.scalar_tensor_tensor(flat(q), e_lv, 1.0, flat(q), ALU.min, ALU.mult).then_inc(s_qk, 1)
                    bb = halves(flat(b), CHUNK)
                    last_b = bb[:, :, CHUNK - 1:CHUNK].broadcast_to([P, HEADS * T // CHUNK, CHUNK])
                    dve.wait_ge(s_qk, 2 * LEVELS + 1)
                    nc.vector.tensor_tensor(halves(e_lv, CHUNK), last_b, bb, ALU.subtract).then_inc(s_e, 1)
                if n == 22:
                    dve.wait_ge(s_exp, LEVELS + 2)
                    nc.vector.scalar_tensor_tensor(flat(k), e_lv, 1.0, flat(k), ALU.min, ALU.mult).then_inc(s_qk, 1)
                if n in (24, 26, 28):
                    c = (n - 24) // 2
                    dve.wait_ge(s_u, c + 1)
                    dve.wait_ge(s_el, 1)
                    if c:
                        dve.wait_ge(s_state, HEADS * c)
                    for hd in range(HEADS):
                        at = hd * DV
                        new = states[:, c + 1, at:at + DV]
                        src = ps[:, 6 + hd // 2, at % 512:at % 512 + DV]
                        if c == 0:
                            nc.vector.tensor_copy(new, src).then_inc(s_state, 1)
                        else:
                            nc.vector.scalar_tensor_tensor(new, states[:, c, at:at + DV], e_last[:, hd, c:c + 1], src,
                                                           ALU.mult, ALU.add).then_inc(s_state, 1)
                heads_of = lambda t: t.rearrange("p (h w) n -> p h w n", w=2)
                if n in (26, 28, 30, 31):
                    c = (26, 28, 30, 31).index(n)
                    dve.wait_ge(s_osq, c + 1)
                    sq = heads_of(v[:, c, :].rearrange("p (a n) -> p a n", n=P))
                    nc.vector.tensor_tensor(sq[:, :, 0, :], sq[:, :, 0, :], sq[:, :, 1, :], ALU.add).then_inc(s_oadd, 1)
                if n == 32:
                    dve.wait_ge(s_osqrt, 1)
                    nc.vector.reciprocal(ro_tok[:, :], ro_tok[:, :]).then_inc(s_ors, 1)
                if n == 33:
                    dve.wait_ge(s_silu, 8)
                    for w in range(2):
                        nc.vector.scalar_tensor_tensor(heads_of(gate[:, :, :])[:, :, w, :], heads_of(o[:, :, :])[:, :, w, :],
                                                       vcol("gla_g", w), heads_of(gate[:, :, :])[:, :, w, :],
                                                       ALU.mult, ALU.mult).then_inc(s_og, 1)
                if n == 34:
                    dve.wait_ge(s_obc, 1)
                    dve.wait_ge(s_og, 2)
                    for half in range(2):
                        rs_heads = ps[:, 4 + 2 * half:6 + 2 * half, :].rearrange("p h (w n) -> p h w n", w=1).broadcast_to([P, 2, 2, T])
                        nc.vector.tensor_tensor(heads_of(o[:, 4 * half:4 * half + 4, :]), heads_of(gate[:, 4 * half:4 * half + 4, :]),
                                                rs_heads, ALU.mult).then_inc(s_mid, 1)

            def m_low(src, kk, mhi_no):
                dve.wait_ge(s_mhi, mhi_no)
                nc.vector.tensor_tensor(m_hl[:, kk % RING, 1, :], src, m_hl[:, kk % RING, 0, :].bitcast(fp32),
                                        ALU.subtract).then_inc(s_mlo, 1)

            def short_conv(m):
                wc = lambda tap: vcol("w_sc", tap * 4 + m)
                dve.wait_ge(s_scv, 1)
                nc.vector.tensor_scalar(y_a[:, m, :], sc_p[:, m, :], wc(2), None, ALU.mult).then_inc(s_scv, 1)
                dve.wait_ge(s_scv, 3 * m + 2)
                nc.vector.scalar_tensor_tensor(y_a[:, m, 1:], sc_p[:, m, :T - 1], wc(1), y_a[:, m, 1:], ALU.mult, ALU.add).then_inc(s_scv, 1)
                dve.wait_ge(s_scv, 3 * m + 3)
                nc.vector.scalar_tensor_tensor(y_a[:, m, 2:], sc_p[:, m, :T - 2], wc(0), y_a[:, m, 2:], ALU.mult, ALU.add).then_inc(s_scv, 1)
                dve.wait_ge(s_scv, 3 * m + 4)
                nc.vector.tensor_tensor(y_a[:, m, :], y_a[:, m, :], q[:, m, :], ALU.mult).then_inc(s_mid, 1)

            for kk in range(3):
                m_low(o[:, kk, :], kk, kk + 1)
            for m in range(4):
                evac("in_proj", 8, m, q[:, m, :], 0)
            dve.wait_ge(s_free, 36)
            short_conv(0)
            short_conv(1)
            m_low(o[:, 3, :], 3, 4)
            short_conv(2)
            short_conv(3)
            for kk in range(4, 8):
                m_low(o[:, kk, :], kk, kk + 1)
            for kk in range(8, 12):
                m_low(y_a[:, kk - 8, :], kk, kk + 1)

            def close(stage, o_idx, gain, gain0, pre, pre0, bias):
                post = 2 * o_idx - 1
                for m in range(KT):
                    if 2 <= m:
                        add_square(m - 1, post)
                    dve.wait_ge(s_xsq, KT * post + m + 1)
                    nc.vector.tensor_scalar(y[:, m, :], ps[:, m, :], vcol(bias, m) if bias else 0.0, vcol(gain, gain0 + m),
                                            ALU.add, ALU.mult).then_inc(s_free, 1)
                inverse_rms(post)
                if o_idx == 1:
                    dve.wait_ge(s_x_again, 16)
                dve.wait_ge(s_bc, post + 1)
                for m in range(KT):
                    nc.vector.tensor_tensor(y[:, m, :], y[:, m, :], ps[:, 7, :], ALU.mult).then_inc(s_yn, 1)
                    dve.wait_ge(s_yn, KT * (o_idx - 1) + m + 1)
                    nc.vector.tensor_tensor(x[:, m, :], x[:, m, :], y[:, m, :], ALU.add).then_inc(s_xnew, 1)
                    if pre and m:
                        h_low(m - 1, o_idx, vcol(pre, pre0 + m - 1))
                        if m > 1:
                            add_square(m - 1, 2 * o_idx)
                if pre:
                    h_low(KT - 1, o_idx, vcol(pre, pre0 + KT - 1))

            def mlp(layer):
                up, down = f"up{layer}", f"down{layer}"
                o_idx = 1 if layer == 0 else 3
                mid_done = 6 if layer == 0 else 6 + HT + KT
                mhi0 = 12 if layer == 0 else 12 + HT + KT
                f_up = FREED[up]

                def evac_group(half, i=None, tile0=0):
                    at = (lambda c, per: c) if i is None else (lambda c, per: i * per + c)
                    g0 = tile0 // 4
                    for m in range(4):
                        dve.wait_ge(s_pe[up], at(narrow_bank_done(g0, m), 14))
                        nc.vector.tensor_tensor(work[m % 2][:, :], ps[:, 4 * half + m, :], rs[:, :], ALU.mult).then_inc(s_free, 1)
                        dve.wait_ge(s_free, at(f_up + tile0 + m + 1, 8))
                        dst = mid[:, tile0 + m, :] if i is None else mid[:, bass.ds(i * 8 + (tile0 + m), 1), :].rearrange("p a n -> p (a n)")
                        nc.vector.scalar_tensor_tensor(dst, work[m % 2][:, :], 0.0, work[m % 2][:, :],
                                                       ALU.max, ALU.mult).then_inc(s_mid, 1)

                inverse_rms(2 * o_idx)
                dve.wait_ge(s_rs, o_idx + 1)
                evac_group(0)
                evac_group(1, tile0=4)
                for kk in range(3):
                    m_low(mid[:, kk, :], kk, mhi0 + kk + 1)
                with dve.Fori(1, 4) as i:
                    evac_group(0, i, 0)
                    evac_group(1, i, 4)
                m_low(mid[:, 3, :], 3, mhi0 + 4)
                with dve.Fori(1, 8) as i:
                    for c in range(4):
                        dve.wait_ge(s_mhi, i * 4 + (mhi0 + c + 1))
                        nc.vector.tensor_tensor(m_hl[:, c, 1, :], mid[:, bass.ds(i * 4 + c, 1), :].rearrange("p a n -> p (a n)"),
                                                m_hl[:, c, 0, :].bitcast(fp32), ALU.subtract).then_inc(s_mlo, 1)
                if layer == 0:
                    close(down, 2, "mlp_post", 0, "mix_pre", KT, None)
                else:
                    close(down, 4, "mlp_post", KT, None, 0, None)

            close("out_proj", 1, "mix_post", 0, "mlp_pre", 0, None)
            mlp(0)

            nc.vector.memset(u[:, :, 0:CF_K - 1], 0.0).then_inc(s_uw, 1)
            inverse_rms(4)
            f = FREED["pw1"]

            def glu(g):
                bank0 = 4 * (g % 2)
                if g:
                    dve.wait_ge(s_u1, 2 * g)
                for m in (2, 3, 0, 1):
                    dve.wait_ge(s_pe["pw1"], narrow_bank_done(g, m))
                    out = sg[:, m - 2, :] if m >= 2 else work[m][:, :]
                    nc.vector.tensor_tensor(out, ps[:, bank0 + m, :], rs[:, :], ALU.mult).then_inc(s_free, 1)
                for m in range(2):
                    c = 2 * g + m
                    dve.wait_ge(s_free, f + 4 * g + 2 + m + 1)
                    dve.wait_ge(s_sig, c + 1)
                    nc.vector.scalar_tensor_tensor(u[:, c, CF_K - 1:], work[m][:, :], vcol("b_pw1", c), sg[:, m, :],
                                                   ALU.add, ALU.mult).then_inc(s_u1, 1)

            def first_taps(c, done):
                dve.wait_ge(s_uw, 1)
                dve.wait_ge(s_u1, c + 2)
                for t in (c, c + 1):
                    nc.vector.tensor_scalar(d[:, t, :], u[:, t, 0:T], vcol("w_dw", t * CF_K), vcol("b_dw", t),
                                            ALU.mult, ALU.add).then_inc(s_cv, 1)

            def taps(c, t0, t1, done):
                with dve.Fori(t0, t1) as i:
                    for t in (0, 1):
                        at = dve.snap(i + (VEC["w_dw"] + (c + t) * CF_K))
                        dve.wait_ge(s_cv, i * 2 + (done - 2 * t0 - 1 + t))
                        nc.vector.scalar_tensor_tensor(d[:, c + t, :], u[:, c + t, bass.ds(i, T)], vec[:, bass.ds(at, 1)],
                                                       d[:, c + t, :], ALU.mult, ALU.add).then_inc(s_cv, 1)

            lo0 = PE_TILES[0] * CF_K
            dve.wait_ge(s_dwhi, 1)
            nc.vector.tensor_tensor(dw_lo[:, :], vec[:, VEC["w_dw"] + lo0:VEC["w_dw"] + KT * CF_K],
                                    dw_hi[:, :].bitcast(fp32), ALU.subtract).then_inc(s_dwlo, 1)
            dve.wait_ge(s_rs, 3)
            glu(0)
            first_taps(0, 0)
            taps(0, 1, 13, 2)
            glu(1)
            taps(0, 13, 25, 26)
            glu(2)
            taps(0, 25, CF_K, 50)
            first_taps(2, 62)
            taps(2, 1, 7, 64)
            glu(3)
            taps(2, 7, CF_K, 76)
            dve.wait_ge(s_dpe, 2)
            taps(4, PE_TAPS[4], CF_K, DONE23)

            dve.wait_ge(s_mean, 1)
            for m in range(KT):
                nc.vector.scalar_tensor_tensor(d[:, m, :], ps[:, 4, :], -1.0 / D, d[:, m, :], ALU.mult, ALU.add).then_inc(s_ln, 1)
            dve.wait_ge(s_lnroot, 1)
            nc.vector.reciprocal(r_tok[:, :], r_tok[:, :]).then_inc(s_lninv, 1)
            dve.wait_ge(s_lnbc, 1)
            for m in range(KT):
                nc.vector.tensor_tensor(d[:, m, :], d[:, m, :], ps[:, 7, :], ALU.mult).then_inc(s_z, 1)
                if m >= 3:
                    m_low(act_d[:, m - 3, :], m - 3, 12 + HT + m - 3 + 1)
            for m in range(KT - 3, KT):
                m_low(act_d[:, m, :], m, 12 + HT + m + 1)
            close("pw2", 3, "mix_post", KT, "mlp_pre", KT, "b_pw2")
            mlp(1)


_INS = ["x_t", "w_in", "w_gk2", "b_gk2", "w_out", "w_pw1", "w_pw2", "w_up", "w_down", "vecs", "squares", "masks"]


def _columns(a):
    return np.ascontiguousarray(a.reshape(-1, P).T)


def _shape_constants():
    j, i = np.arange(P)[:, None], np.arange(P)[None, :]
    tri = (j <= i) / GATE_NORM
    squares = np.stack([np.ones((P, P)), np.eye(P), tri], axis=1).astype(np.float32)
    levels = []
    for lv in range(LEVELS):
        s = CHUNK >> lv
        n = np.arange(HALF)
        row = (n // (s // 2)) * s + s // 2 + n % (s // 2)
        levels.append((j // s == row // s) & (j % s < s // 2))
    return squares, np.concatenate([*levels, j == i], axis=1).astype(np.float32)


def kernel(**inputs):
    import concourse.bacc as bacc
    from concourse.bass_utils import run_bass_kernel_spmd

    a = {n: np.asarray(t) for n, t in inputs.items()}
    squares, masks = _shape_constants()
    dw = a["cf_w_dw"][0].reshape(CF_K, KT, P).transpose(1, 0, 2).reshape(-1)
    parts = [a["norm_mix_pre"], a["norm_mix_post"], a["norm_mlp_pre"], a["norm_mlp_post"], a["cf_b_pw1"], a["cf_b_dw"],
             a["cf_ln_g"], a["cf_ln_b"], a["cf_b_pw2"], a["gla_norm_g"], a["sc_w_conv"], dw]
    cols = [_columns(p) for p in parts]
    cols += [np.full((P, 1), EPS, np.float32), np.zeros((P, 1), np.float32)]
    pw1 = a["cf_w_pw1"][0].reshape(D, 2, 4, D // 4).transpose(0, 2, 1, 3).reshape(D, 2 * D)
    arrays = {"x_t": a["x"][0].T, "w_in": a["ab_w_in"][0], "w_gk2": a["gla_w_gk2"][0], "b_gk2": a["gla_b_gk2"],
              "w_out": a["ab_w_out"][0], "w_pw1": pw1, "w_pw2": a["cf_w_pw2"][0],
              "w_up": a["mlp_w1"], "w_down": a["mlp_w2"], "vecs": np.concatenate(cols, axis=1),
              "squares": squares, "masks": masks}
    arrays = {n: np.ascontiguousarray(t) for n, t in arrays.items()}
    nc = bacc.Bacc("TRN2", target_bir_lowering=False, num_devices=1)
    args = [nc.dram_tensor(n, arrays[n].shape, mybir.dt.from_np(arrays[n].dtype), kind="ExternalInput").ap() for n in _INS]
    out_t = nc.dram_tensor("out_t", (D, T), mybir.dt.float32, kind="ExternalOutput").ap()
    build(nc, *args, out_t)
    r = run_bass_kernel_spmd(nc, [arrays], core_ids=[0])
    return np.ascontiguousarray(np.asarray(r.results[0]["out_t"]).T)[None]
```

```python
from contextlib import ExitStack

import concourse.bass as bass
import numpy as np
from concourse import mybir

P = 128
D = 1024
T = 512
KT = D // P
CHUNK = 128
HALF = CHUNK // 2
HEADS = 4
DK = D // 2 // HEADS
DV = D // HEADS
RANK = 16
SCW = D // 2
GATE_NORM = 16.0
CF_K = 31
HID = 4 * D
HT = HID // P
EPS = 1e-6
CP = T // P
LEVELS = 7
SUMMED_TILE = 3
SUMMED_TAPS = 20
PE_TILES = range(5, KT)
PE_TAPS = {5: SUMMED_TAPS, 6: CF_K, 7: CF_K}
BATCH = 4

VEC_SIZES = [("mix_pre", 2 * KT), ("mix_post", 2 * KT), ("mlp_pre", 2 * KT), ("mlp_post", 2 * KT),
             ("b_pw1", 2 * KT), ("b_dw", KT), ("ln_g", KT), ("ln_b", KT), ("b_pw2", KT),
             ("gla_g", DV // P), ("w_sc", 3 * SCW // P), ("w_dw", CF_K * KT), ("eps", 1)]
VEC, _at = {}, 0
for _name, _n in VEC_SIZES:
    VEC[_name] = _at
    _at += _n
NVEC = _at

STAGES = [("in_proj", 36), ("out_proj", 12), ("up0", 32), ("down0", 32), ("pw1", 16), ("pw2", 8),
          ("up1", 32), ("down1", 32)]
FIRST, _at = {}, 0
for _name, _n in STAGES:
    FIRST[_name] = _at
    _at += _n
STEPS = dict(STAGES)
TOTAL_STEPS = _at
RING = 4
AHEAD = 3


def build(nc, x_t, w_in, w_gk2, b_gk2, w_out, w_pw1, w_pw2, w_up, w_down, vecs, squares, masks, out_t):
    fp32, f32r, u8 = mybir.dt.float32, mybir.dt.float32r, mybir.dt.uint8
    ALU, ACT = mybir.AluOpType, mybir.ActivationFunctionType
    ctx = ExitStack()
    with ctx:
        def sb(name, shape, dt=fp32):
            return ctx.enter_context(nc.sbuf_tensor(name, shape, dt))

        def sem(name):
            return ctx.enter_context(nc.semaphore(name))

        x = sb("x", [P, KT, T])
        raw = [sb(f"raw{i}", [P, D]) for i in range(RING)]
        w_hi = [sb(f"w_hi{i}", [P, D], f32r) for i in range(RING)]
        w_lo = [sb(f"w_lo{i}", [P, D], f32r) for i in range(RING)]
        h_hi = sb("h_hi", [P, KT, T], f32r)
        h_lo = sb("h_lo", [P, KT, T], f32r)
        y = sb("y", [P, KT, T])
        vec = sb("vec", [P, NVEC])
        sq_const = sb("sq_const", [P, 3, P])
        mask = sb("mask", [P, LEVELS * HALF + P], u8)
        acc = sb("acc", [P, T])
        work = [sb(f"work{i}", [P, T]) for i in range(2)]
        rs = sb("rs", [P, T])
        r_tok = sb("r_tok", [P, CP])
        ro_tok = sb("ro_tok", [P, HEADS * CP])
        e_last = sb("e_last", [P, HEADS, T // CHUNK])
        w_lr = sb("w_lr", [P, KT, RANK])
        with nc.sbuf_tensor("gate", [P, 2 * HEADS, T], fp32) as gate:
            pass
        m_hl = sb("m_hl", [P, RING, 2, T], f32r)
        with ExitStack() as over:
            def mx(name, shape, dt=fp32):
                return over.enter_context(nc.sbuf_tensor(name, shape, dt))
            y_a = mx("y_a", [P, SCW // P, T])
            o = mx("o", [P, 2 * HEADS, T])
            q = mx("q", [P, HEADS, T])
            k = mx("k", [P, HEADS, T])
            b = mx("b", [P, HEADS, T])
            v = mx("v", [P, CP, HEADS * DV])
        with ExitStack() as over:
            def mx(name, shape, dt=fp32):
                return over.enter_context(nc.sbuf_tensor(name, shape, dt))
            u = mx("u", [P, KT, CF_K - 1 + T])
            d = mx("d", [P, KT, T])
            sg = mx("sg", [P, 2, T])
            diag = mx("diag", [P, 2, 2, BATCH, P], f32r)
            dw_hi = mx("dw_hi", [P, len(PE_TILES) * CF_K], f32r)
            dw_lo = mx("dw_lo", [P, len(PE_TILES) * CF_K])
            with nc.sbuf_tensor("act_d", [P, KT, T], fp32) as act_d:
                pass
            u_hl = mx("u_hl", [P, len(PE_TILES), 2, CF_K - 1 + T], f32r)
        mid = sb("mid", [P, HT, T])

        scores = x[:, 0:4, :].rearrange("p a (c i) -> p (a c) i", i=P)
        q_lv = x[:, 4:6, :].rearrange("p a n -> p (a n)")
        e_lv = o[:, 0:4, :].rearrange("p a n -> p (a n)")
        k_lv = o[:, 4:8, :]
        g_tok = o[:, 0:4, :]
        softp = o[:, 4:8, :]
        kd_tok = b
        sc_p = k
        lr = y[0:RANK + 1, 0, :]
        wgk2 = y[0:RANK + 1, 1, :]
        mask_in = y[:, 2:4, :].rearrange("p a n -> p (a n)")[:, 0:LEVELS * HALF + P]
        states = y[:, :, :].rearrange("p (s a) n -> p s (a n)", s=RING)
        products = y[:, 0:RING, :]
        ones = sq_const[:, 0, :]
        ident = sq_const[:, 1, :]
        tri = sq_const[:, 2, :]

        ps = ctx.enter_context(nc.psum_tensor("ps", [P, 8, 512], fp32))

        def vcol(name, c):
            return vec[:, VEC[name] + c:VEC[name] + c + 1]

        eps = vcol("eps", 0)

        s_vec = sem("s_vec")
        s_const = sem("s_const")
        s_lr_in = sem("s_lr_in")
        s_gk_in = sem("s_gk_in")
        s_x = [sem(f"s_x{i}") for i in range(KT)]
        s_x_again = sem("s_x_again")
        s_raw = [sem(f"s_raw{i}") for i in range(RING)]
        s_out = sem("s_out")
        s_whi = sem("s_whi")
        s_wlo = sem("s_wlo")
        s_pe = {n: sem(f"s_pe_{n}") for n, _ in STAGES}
        s_free = sem("s_free")
        s_hhi = sem("s_hhi")
        s_hlo = sem("s_hlo")
        s_mid = sem("s_mid")
        s_mhi = sem("s_mhi")
        s_mlo = sem("s_mlo")
        s_xsq = sem("s_xsq")
        s_acc = sem("s_acc")
        s_ss = sem("s_ss")
        s_sqrt = sem("s_sqrt")
        s_inv = sem("s_inv")
        s_bc = sem("s_bc")
        s_rs = sem("s_rs")
        s_yn = sem("s_yn")
        s_xnew = sem("s_xnew")
        s_xlast = sem("s_xlast")
        s_warm = sem("s_warm")
        s_warm_pe = sem("s_warm_pe")
        s_qn = sem("s_qn")
        s_set = sem("s_set")
        s_lrp = sem("s_lrp")
        s_lr = sem("s_lr")
        s_gkp = sem("s_gkp")
        s_sp = sem("s_sp")
        s_g = sem("s_g")
        s_bp = sem("s_bp")
        s_b = sem("s_b")
        s_e = sem("s_e")
        s_exp = sem("s_exp")
        s_el = sem("s_el")
        s_qk = sem("s_qk")
        s_sc = sem("s_sc")
        s_pred = sem("s_pred")
        s_kdp = sem("s_kdp")
        s_kd = sem("s_kd")
        s_u = sem("s_u")
        s_state = sem("s_state")
        s_op = sem("s_op")
        s_o = sem("s_o")
        s_osq = sem("s_osq")
        s_oadd = sem("s_oadd")
        s_oss = sem("s_oss")
        s_osqrt = sem("s_osqrt")
        s_ors = sem("s_ors")
        s_obc = sem("s_obc")
        s_silu = sem("s_silu")
        s_og = sem("s_og")
        s_scv = sem("s_scv")
        s_sig = sem("s_sig")
        s_uw = sem("s_uw")
        s_u1 = sem("s_u1")
        s_cv = sem("s_cv")
        s_dwhi = sem("s_dwhi")
        s_dwlo = sem("s_dwlo")
        s_uhi = sem("s_uhi")
        s_ulo = sem("s_ulo")
        s_diagw = sem("s_diagw")
        s_diagl = sem("s_diagl")
        s_tap = sem("s_tap")
        s_dpe = sem("s_dpe")
        s_prod = sem("s_prod")
        s_padd = sem("s_padd")
        s_dsum = sem("s_dsum")
        s_mean = sem("s_mean")
        s_ln = sem("s_ln")
        s_lnsq = sem("s_lnsq")
        s_lnadd = sem("s_lnadd")
        s_lnss = sem("s_lnss")
        s_lnroot = sem("s_lnroot")
        s_lninv = sem("s_lninv")
        s_lnbc = sem("s_lnbc")
        s_z = sem("s_z")

        block = ctx.enter_context(nc.Block())

        def narrow_step_done(step):
            g, j = divmod(step, 4)
            return 7 * g + (j + 1 if j < 3 else 7)

        def narrow_bank_done(g, m):
            return 7 * g + 3 + m + 1

        def wide_bank_done(stage, m):
            return STEPS[stage] - 2 + m + 1

        WIDE = ("out_proj", "down0", "pw2", "down1")
        FREED, freed = {}, 0
        for stage, steps in STAGES:
            FREED[stage] = freed
            freed += KT if stage in WIDE else steps
        MID_DONE = {"down0": 6, "pw2": 6 + HT, "down1": 6 + HT + KT}
        SPLIT_DONE = {"out_proj": 0, "down0": 12, "pw2": 12 + HT, "down1": 12 + HT + KT}
        LAST_POOL = (1, 3, 5)
        GLU_READ = {2: 1, 3: 2, 0: 3, 1: 4}
        BATCHES = [(c, t0, min(BATCH, PE_TAPS[c] - t0)) for c in PE_TILES for t0 in range(0, PE_TAPS[c], BATCH)]
        TILE_END = {c: sum(1 for no in BATCHES if no[0] <= c) for c in PE_TILES}
        DONE01, DONE24 = 2 * CF_K, 4 * CF_K
        CONV_DVE = DONE24 + 2 * CF_K - PE_TAPS[5] - SUMMED_TAPS
        EARLY_TAPS = {n: (2 * (n - 10) + 1, 2 * (n - 10) + 2) for n in range(10, 15)}
        LATE_TAP = {no: no + 8 for no in range(3, 3 + SUMMED_TAPS - 11)}
        ORDER = [n for n, _ in STAGES]

        @block.sync
        def _(sp):
            def narrow_group(w, g0, col, i=None, n=0):
                for j in range(4):
                    step = g0 + j if i is None else None
                    src = w[256 * j:256 * j + 256, bass.ds(col, 512)].rearrange("(a p) n -> p a n", p=P)
                    if i is None:
                        if step >= RING:
                            sp.wait_ge(s_wlo, step - RING + 1)
                    else:
                        sp.wait_ge(s_wlo, i * n + (g0 + j - RING + 1))
                    sp.dma_start(raw[j][:, :].rearrange("p (a n) -> p a n", a=2), src).then_inc(s_raw[j], 16)

            cols = [1536, 2048, 2560, 3072, 3584, 4096, 0, 1024, 512]
            for j in range(4):
                sp.dma_start(raw[j][:, :].rearrange("p (a n) -> p a n", a=2),
                             w_in[256 * j:256 * j + 256, cols[0]:cols[0] + 512].rearrange("(a p) n -> p a n", p=P)).then_inc(s_raw[j], 16)
                for m in (2 * j, 2 * j + 1):
                    sp.dma_start(x[:, m, :], x_t[m * P:(m + 1) * P, :]).then_inc(s_x[m], 16)
            sp.dma_start(sq_const[:, :, :], squares).then_inc(s_const, 16)
            sp.dma_start(mask_in, masks).then_inc(s_const, 16)
            sp.dma_start(w_lr[:, :, :], w_in[:, 4608:4624].rearrange("(a p) n -> p a n", p=P)).then_inc(s_lr_in, 16)
            sp.dma_start(wgk2[0:RANK, :], w_gk2).then_inc(s_gk_in, 16)
            sp.dma_start(wgk2[RANK:RANK + 1, :], b_gk2).then_inc(s_gk_in, 16)
            for g in range(1, 9):
                narrow_group(w_in, 4 * g, cols[g])

            def wide(stage, w, row0, k0, k1):
                base = FIRST[stage]
                with sp.Fori(k0 // 4, k1 // 4) as i:
                    for s in range(4):
                        row = sp.snap(i * 512 + (row0 + s * P))
                        sp.wait_ge(s_wlo, i * 4 + (base + s - RING + 1))
                        sp.dma_start(raw[s][:, :], w[bass.ds(row, P), :]).then_inc(s_raw[s], 16)

            wide("out_proj", w_out, SCW, 0, 8)
            wide("out_proj", w_out, -8 * P, 8, 12)
            sp.wait_ge(s_op, CP)
            sp.dma_start(x[:, :, :], x_t.rearrange("(a p) n -> p a n", p=P)).then_inc(s_x_again, 16)

            def mlp(layer):
                with sp.Fori(0, 8) as i:
                    col = sp.snap(i * 512)
                    narrow_group(w_up[layer], FIRST[f"up{layer}"], col, i, 4)
                wide(f"down{layer}", w_down[layer], 0, 0, HT)

            mlp(0)
            for g in range(4):
                narrow_group(w_pw1, FIRST["pw1"] + 4 * g, 512 * g)
            wide("pw2", w_pw2, 0, 0, KT)
            mlp(1)
            for m in range(KT):
                if m in LAST_POOL:
                    sp.wait_ge(s_xlast, LAST_POOL.index(m) + 1)
                else:
                    sp.wait_ge(s_xnew, 3 * KT + m + 1 - sum(n < m for n in LAST_POOL))
                sp.dma_start(out_t[m * P:(m + 1) * P, :], x[:, m, :]).then_inc(s_out, 16)
            sp.wait_ge(s_out, 16 * KT)

        @block.gpsimd
        def _(pool):
            def low_part(s, count):
                pool.wait_ge(s_whi, count)
                nc.gpsimd.tensor_tensor(w_lo[s][:, :], raw[s][:, :], w_hi[s][:, :].bitcast(fp32),
                                        ALU.subtract).then_inc(s_wlo, 1)

            def low_parts(first, last):
                for step in range(first, last):
                    low_part(step % RING, step + 1)

            def low_parts_loop(first, last):
                with pool.Fori(first // RING, last // RING) as i:
                    for s in range(RING):
                        low_part(s, i * RING + (s + 1))

            def u_low(c):
                pool.wait_ge(s_uhi, c - PE_TILES[0] + 1)
                hl = u_hl[:, c - PE_TILES[0], :, :]
                nc.gpsimd.tensor_tensor(hl[:, 1, :], u[:, c, :], hl[:, 0, :].bitcast(fp32), ALU.subtract).then_inc(s_ulo, 1)

            def diagonals(no):
                c, t0, n = BATCHES[no]
                if no >= 2:
                    pool.wait_ge(s_tap, no - 1)
                at = (c - PE_TILES[0]) * CF_K + t0
                nc.gpsimd.tensor_tensor(diag[:, no % 2, 0, 0:n, :],
                                        ident.rearrange("p (a i) -> p a i", a=1).broadcast_to([P, n, P]),
                                        dw_hi[:, at:at + n].bitcast(fp32).rearrange("p (t a) -> p t a", a=1).broadcast_to([P, n, P]),
                                        ALU.mult).then_inc(s_diagw, 1)

            def add_tap(t):
                pool.wait_ge(s_prod, t + 1)
                if t > 1:
                    pool.wait_ge(s_padd, t - 1)
                nc.gpsimd.tensor_tensor(d[:, SUMMED_TILE, :], d[:, SUMMED_TILE, :], products[:, t % RING, :], ALU.add).then_inc(s_padd, 1)

            def d_sum(n, first, second, ready):
                if n > 1:
                    pool.wait_ge(s_dsum, n - 1)
                pool.wait_ge(*ready)
                nc.gpsimd.tensor_tensor(acc[:, :], first, d[:, second, :], ALU.add).then_inc(s_dsum, 1)

            pw2 = FIRST["pw2"]
            low_parts_loop(0, pw2 - 8)
            low_parts(pw2 - 8, pw2 - 4)
            pool.wait_ge(s_dwhi, 1)
            diagonals(0)
            diagonals(1)
            for step in range(pw2 - 4, pw2 + AHEAD):
                low_parts(step, step + 1)
                if step == pw2 - 1:
                    u_low(5)
                for t in EARLY_TAPS.get(step - AHEAD - FIRST["pw1"], ()):
                    add_tap(t)
            for no in range(2, len(BATCHES)):
                diagonals(no)
                if no in LATE_TAP:
                    add_tap(LATE_TAP[no])
                if no == 4:
                    u_low(6)
                if no == 8:
                    u_low(7)
                if no == 10:
                    d_sum(1, d[:, 0, :], 1, (s_cv, DONE01))
                if no == len(BATCHES) - 5:
                    d_sum(2, acc[:, :], 6, (s_dpe, 2))
                if no == len(BATCHES) - 3:
                    d_sum(3, acc[:, :], 2, (s_cv, DONE24))
                if no == len(BATCHES) - 2:
                    d_sum(4, acc[:, :], 4, (s_cv, DONE24))
            for pair in (1, 2):
                pool.wait_ge(s_lnsq, 2 * pair + 2)
                nc.gpsimd.tensor_tensor(act_d[:, 2 * pair, :], act_d[:, 2 * pair, :], act_d[:, 2 * pair + 1, :],
                                        ALU.add).then_inc(s_lnadd, 1)
            low_parts(pw2 + AHEAD, pw2 + RING)
            low_parts_loop(pw2 + RING, TOTAL_STEPS)
            for m in LAST_POOL:
                pool.wait_ge(s_yn, 3 * KT + m + 1)
                nc.gpsimd.tensor_tensor(x[:, m, :], x[:, m, :], y[:, m, :], ALU.add).then_inc(s_xlast, 1)

        @block.scalar
        def _(act):
            def w_high(step):
                s = step % RING
                act.wait_ge(s_raw[s], 16 * (step // RING + 1))
                if step >= RING:
                    free = step - RING
                    stage = [n for n in ORDER if FIRST[n] <= free][-1]
                    local = free - FIRST[stage]
                    last = local >= STEPS[stage] - 2
                    done = narrow_step_done(local) if stage not in WIDE else (
                        wide_bank_done(stage, 7) if last else local + 1)
                    act.wait_ge(s_pe[stage], done)
                nc.scalar.activation(w_hi[s][:, :], raw[s][:, :], ACT.Copy).then_inc(s_whi, 1)

            def m_high(src, kk, ready, slot_free):
                if ready is not None:
                    act.wait_ge(*ready)
                if slot_free is not None:
                    act.wait_ge(*slot_free)
                nc.scalar.activation(m_hl[:, kk % RING, 0, :], src, ACT.Copy).then_inc(s_mhi, 1)

            act.dma_start(vec[:, :], vecs).then_inc(s_vec, 16)
            act.wait_ge(s_warm, 1)
            nc.scalar.activation(r_tok[:, :], r_tok[:, :], ACT.Sqrt).then_inc(s_warm, 1)
            act.wait_ge(s_vec, 16)

            def open_tile(m, o_idx, gain, ready):
                act.wait_ge(*ready)
                nc.scalar.activation(h_hi[:, m, :], x[:, m, :], ACT.Copy, scale=gain).then_inc(s_hhi, 1)
                square_tile(m, 2 * o_idx, x)

            def square_tile(m, norm, src, bias=0.0):
                if m >= 3:
                    act.wait_ge(s_acc, 6 * norm + m - 2)
                dst = acc if m == 0 else work[m % 2]
                nc.scalar.activation(dst[:, :], src[:, m, :], ACT.Square, bias=bias).then_inc(s_xsq, 1)

            for m in range(KT):
                if m < 3:
                    w_high(m)
                open_tile(m, 0, vcol("mix_pre", m), (s_x[m], 16))

            def root(norm, sums):
                act.wait_ge(s_ss, norm + 1)
                nc.scalar.activation(r_tok[:, :], sums, ACT.Sqrt, bias=eps, scale=1.0 / D).then_inc(s_sqrt, 1)

            def keep_rs(norm):
                act.wait_ge(s_bc, norm + 1)
                if norm == 0:
                    act.wait_ge(s_warm_pe, 2)
                nc.scalar.activation(rs[:, :], ps[:, 7, :], ACT.Copy).then_inc(s_rs, 1)

            for n in range(36):
                if n == 4:
                    root(0, ps[:, 6, 0::P])
                w_high(n + AHEAD)
                if n == 5:
                    keep_rs(0)
                if n == 7:
                    act.wait_ge(s_gkp, 1)
                    nc.scalar.activation(softp, ps[:, 4:8, :], ACT.Abs).then_inc(s_sp, 1)
                    act.wait_ge(s_sp, 1)
                    nc.scalar.activation(softp, softp, ACT.Exp, scale=-1.0).then_inc(s_sp, 1)
                    act.wait_ge(s_sp, 2)
                    nc.scalar.activation(softp, softp, ACT.Ln, bias=1.0).then_inc(s_sp, 1)
                if n == 10:
                    act.wait_ge(s_bp, 1)
                    nc.scalar.activation(b[:, :, :], ps[:, 4:8, :], ACT.Copy).then_inc(s_b, 1)
                if 13 <= n < 13 + LEVELS:
                    act.wait_ge(s_e, 2 * (n - 13) + 2)
                    nc.scalar.activation(e_lv, e_lv, ACT.Exp).then_inc(s_exp, 1)
                if n == 20:
                    act.wait_ge(s_qk, 2 * LEVELS)
                    nc.scalar.activation(e_lv, b[:, :, :].rearrange("p a n -> p (a n)"), ACT.Exp).then_inc(s_exp, 1)
                    nc.scalar.activation(e_last[:, :, :], b[:, :, CHUNK - 1::CHUNK], ACT.Exp).then_inc(s_el, 1)
                if n == 21:
                    act.wait_ge(s_e, 2 * LEVELS + 1)
                    nc.scalar.activation(e_lv, e_lv, ACT.Exp).then_inc(s_exp, 1)
                if n == 23:
                    act.wait_ge(s_kdp, 1)
                    nc.scalar.activation(kd_tok[:, :, :], ps[:, 4:8, :], ACT.Copy).then_inc(s_kd, 1)
                if n in (22, 25):
                    for t in range(4):
                        c = t + (4 if n == 25 else 0)
                        act.wait_ge(s_free, 16 + c + 1)
                        nc.scalar.activation(gate[:, c, :], gate[:, c, :], ACT.Silu).then_inc(s_silu, 1)
                if n in (25, 27, 29, 31):
                    c = (n - 25) // 2
                    act.wait_ge(s_op, c + 1)
                    nc.scalar.activation(o[:, :, c * P:(c + 1) * P],
                                         ps[:, 4:6, :].rearrange("p a (c n) -> p (a c) n", n=P), ACT.Copy).then_inc(s_o, 1)
                    act.wait_ge(s_o, c + 1)
                    nc.scalar.activation(v[:, c, :].rearrange("p (a n) -> p a n", n=P), o[:, :, c * P:(c + 1) * P],
                                         ACT.Square).then_inc(s_osq, 1)
                if n == 32:
                    act.wait_ge(s_oss, 1)
                    nc.scalar.activation(ro_tok[:, :], ps[:, 4, 0:HEADS * CP], ACT.Sqrt, bias=eps, scale=1.0 / DV).then_inc(s_osqrt, 1)

            def wide_stage(stage, tiles, mid0, ready):
                base = FIRST[stage]
                for kk in range(3):
                    m_high(tiles(kk), mid0 + kk, ready(kk), None)
                n = STEPS[stage]
                for kk in range(n):
                    if kk < n - 1:
                        w_high(base + kk + AHEAD)
                    if kk + 3 < n:
                        m_high(tiles(kk + 3), mid0 + kk + 3, ready(kk + 3), (s_pe[stage], kk) if kk else None)

            def close(stage, o_idx, pre):
                post = 2 * o_idx - 1
                for m in range(KT):
                    act.wait_ge(s_pe[stage], wide_bank_done(stage, m))
                    square_tile(m, post, ps, vcol("b_pw2", m) if stage == "pw2" else 0.0)
                root(post, ps[:, 0:CP, 0])
                if pre:
                    after = FIRST[stage] + STEPS[stage]
                    w_high(after + AHEAD - 1)
                    for m in range(KT):
                        if m == 2:
                            w_high(after + AHEAD)
                        open_tile(m, o_idx, vcol(pre[0], pre[1] + m), (s_xnew, KT * (o_idx - 1) + m + 1))

            out_tiles = [o[:, c, :] for c in range(8)] + [y_a[:, c, :] for c in range(4)]
            wide_stage("out_proj", lambda kk: out_tiles[kk], 0,
                       lambda kk: (s_mid, 1 if kk < 2 else 2) if kk < 8 else (s_mid, 2 + kk - 7))
            close("out_proj", 1, ("mlp_pre", 0))

            def mlp(layer):
                up, down = f"up{layer}", f"down{layer}"
                o_idx = 1 if layer == 0 else 3
                mid_done, mhi0 = MID_DONE[down], SPLIT_DONE[down]
                u0, d0 = FIRST[up], FIRST[down]
                for n in range(8):
                    if n == 4:
                        root(2 * o_idx, ps[:, 7, 0::P])
                    if n:
                        w_high(u0 + n + AHEAD)
                    if n == 4:
                        keep_rs(2 * o_idx)
                for kk in range(3):
                    m_high(mid[:, kk, :], kk, (s_mid, mid_done + kk + 1), None)
                with act.Fori(1, 4) as i:
                    for n in range(8):
                        s = (n + AHEAD) % RING
                        act.wait_ge(s_raw[s], i * 32 + 16 * ((u0 + n + AHEAD) // RING + 1))
                        if n == 0:
                            act.wait_ge(s_pe[up], i * 14)
                        else:
                            act.wait_ge(s_pe[up], i * 14 + narrow_step_done(n - 1))
                        nc.scalar.activation(w_hi[s][:, :], raw[s][:, :], ACT.Copy).then_inc(s_whi, 1)
                for kk in range(4):
                    w_high(d0 + kk + AHEAD)
                    m_high(mid[:, kk + 3, :], kk + 3, (s_mid, mid_done + kk + 4), (s_pe[down], kk) if kk else None)
                with act.Fori(1, 7) as i:
                    for c in range(4):
                        s = (c + AHEAD) % RING
                        act.wait_ge(s_raw[s], i * 16 + 16 * ((d0 + c + AHEAD) // RING + 1))
                        act.wait_ge(s_pe[down], i * 4 + c)
                        nc.scalar.activation(w_hi[s][:, :], raw[s][:, :], ACT.Copy).then_inc(s_whi, 1)
                        act.wait_ge(s_mid, i * 4 + (mid_done + c + 4))
                        nc.scalar.activation(m_hl[:, s, 0, :], mid[:, bass.ds(i * 4 + (c + 3), 1), :].rearrange("p a n -> p (a n)"),
                                             ACT.Copy).then_inc(s_mhi, 1)
                for kk in range(28, 32):
                    if d0 + kk + AHEAD < TOTAL_STEPS and kk < HT - 1:
                        w_high(d0 + kk + AHEAD)
                    if kk + 3 < HT:
                        m_high(mid[:, kk + 3, :], kk + 3, (s_mid, mid_done + kk + 4), (s_pe[down], kk))
                close(down, o_idx + 1, ("mix_pre", KT) if layer == 0 else None)

            mlp(0)

            def sigmoids(g):
                for t in range(2):
                    act.wait_ge(s_free, FREED["pw1"] + 4 * g + t + 1)
                    nc.scalar.activation(sg[:, t, :], sg[:, t, :], ACT.Sigmoid, bias=vcol("b_pw1", KT + 2 * g + t)).then_inc(s_sig, 1)

            def u_high(c):
                act.wait_ge(s_uw, 1)
                act.wait_ge(s_u1, c + 1)
                nc.scalar.activation(u_hl[:, c - PE_TILES[0], 0, :], u[:, c, :], ACT.Copy).then_inc(s_uhi, 1)

            def low_diagonals(no):
                c, t0, n = BATCHES[no]
                act.wait_ge(s_dwlo, 1)
                if no >= 2:
                    act.wait_ge(s_tap, no - 1)
                for t in range(n):
                    at = (c - PE_TILES[0]) * CF_K + t0 + t
                    last = nc.scalar.activation(diag[:, no % 2, 1, t, :], ident, ACT.Copy, scale=dw_lo[:, at:at + 1])
                last.then_inc(s_diagl, 1)

            def tap_product(t):
                if t > RING:
                    act.wait_ge(s_padd, t - RING)
                nc.scalar.activation(products[:, t % RING, :], u[:, SUMMED_TILE, t:t + T], ACT.Copy,
                                     scale=vcol("w_dw", SUMMED_TILE * CF_K + t)).then_inc(s_prod, 1)

            def move_d(c):
                act.wait_ge(s_tap, TILE_END[c])
                nc.scalar.activation(d[:, c, :], ps[:, c - PE_TILES[0], :], ACT.Identity, bias=vcol("b_dw", c)).then_inc(s_dpe, 1)

            p0 = FIRST["pw1"]
            for n in range(16):
                if n == 4:
                    root(4, ps[:, 7, 0::P])
                if n:
                    w_high(p0 + n + AHEAD)
                if n == 4:
                    keep_rs(4)
                if n == 2:
                    nc.scalar.activation(dw_hi[:, :], vec[:, VEC["w_dw"] + PE_TILES[0] * CF_K:VEC["w_dw"] + KT * CF_K],
                                         ACT.Copy).then_inc(s_dwhi, 1)
                if n in (5, 9, 13):
                    sigmoids(n // 4 - 1)
                if n == 8:
                    low_diagonals(0)
                    low_diagonals(1)
                if n == 13:
                    u_high(5)
                if n == 10:
                    act.wait_ge(s_uw, 1)
                    act.wait_ge(s_u1, SUMMED_TILE + 1)
                    nc.scalar.activation(d[:, SUMMED_TILE, :], u[:, SUMMED_TILE, 0:T], ACT.Identity,
                                         bias=vcol("b_dw", SUMMED_TILE), scale=vcol("w_dw", SUMMED_TILE * CF_K)).then_inc(s_prod, 1)
                for t in EARLY_TAPS.get(n, ()):
                    tap_product(t)
            sigmoids(3)
            for no in range(2, len(BATCHES)):
                low_diagonals(no)
                if no in (2, 3):
                    u_high(no + 4)
                if no in LATE_TAP:
                    tap_product(LATE_TAP[no])
                for c in PE_TILES:
                    if no == TILE_END[c] + 1:
                        move_d(c)
            move_d(PE_TILES[-1])
            for m in range(KT):
                act.wait_ge(s_ln, m + 1)
                nc.scalar.activation(act_d[:, m, :], d[:, m, :], ACT.Square).then_inc(s_lnsq, 1)
            act.wait_ge(s_lnss, 1)
            nc.scalar.activation(r_tok[:, :], ps[:, 0:CP, 0], ACT.Sqrt, bias=eps, scale=1.0 / D).then_inc(s_lnroot, 1)

            def silu_tile(m):
                act.wait_ge(s_z, m + 1)
                nc.scalar.activation(act_d[:, m, :], d[:, m, :], ACT.Silu, bias=vcol("ln_b", m),
                                     scale=vcol("ln_g", m)).then_inc(s_mid, 1)

            mid0 = MID_DONE["pw2"]
            for m in range(3):
                silu_tile(m)
                m_high(act_d[:, m, :], m, (s_mid, mid0 + m + 1), None)
            q0 = FIRST["pw2"]
            for kk in range(KT):
                if kk < KT - 1:
                    w_high(q0 + kk + AHEAD)
                if kk + 3 < KT:
                    silu_tile(kk + 3)
                    m_high(act_d[:, kk + 3, :], kk + 3, (s_mid, mid0 + kk + 4), (s_pe["pw2"], kk) if kk else None)
            close("pw2", 3, ("mlp_pre", KT))
            mlp(1)

        @block.tensor
        def _(pe):
            PASSES = ((0, 0), (1, 0), (0, 1))
            WARM_START, WARM_ROOT, WARM_NEXT_H, WARM_MEAN, WARM_SILU = 14, 3, 9, 8, 9

            def h(kk, part):
                return (h_hi, h_lo)[part][:, kk, :]

            def wt(s, part, c, n=P):
                return (w_hi, w_lo)[part][s][:, c:c + n]

            def narrow_group(stage, g, bank0, step_of, bank_free, tokens_out=False, after=None, opening=None, norm=None):
                def product(j, kk, m, passes):
                    c = (kk % 2) * 512
                    for n in passes:
                        wp, hp = PASSES[n]
                        if tokens_out:
                            lhs, rhs = h(kk, hp)[:, m * P:(m + 1) * P], wt(j, wp, c, 512)
                        else:
                            lhs, rhs = wt(j, wp, c + m * P), h(kk, hp)
                        last = nc.tensor.matmul(ps[:, bank0 + m, :], lhs, rhs,
                                                start=(kk == 0 and n == 0), stop=(kk == KT - 1 and n == 2))
                    return last

                for j in range(4):
                    if opening is None:
                        pe.wait_ge(s_wlo, step_of(j))
                    pair = (2 * j, 2 * j + 1)
                    if norm is not None and j == 0:
                        for kk in pair:
                            for m in range(3):
                                if kk == 0 and bank_free(m) is not None:
                                    pe.wait_ge(s_free, bank_free(m))
                                product(j, kk, m, (0, 1, 2))
                            if kk == 0:
                                broadcast(norm)
                        pe.wait_ge(s_rs, norm // 2 + 1)
                        pe.wait_ge(s_free, bank_free(3))
                        for kk in pair:
                            last = product(j, kk, 3, (0, 1, 2))
                        last.then_inc(s_pe[stage], 1)
                        continue
                    for kk in pair:
                        for part in (((0,), (1,), (2,)) if opening is not None else ((0, 1, 2),)):
                            if opening is not None:
                                if part[0] == 0:
                                    pe.wait_ge(s_whi, step_of(j))
                                    pe.wait_ge(s_hhi, KT * opening + kk + 1)
                                elif part[0] == 1:
                                    pe.wait_ge(s_wlo, step_of(j))
                                else:
                                    pe.wait_ge(s_hlo, KT * opening + kk + 1)
                            for m in range(4):
                                if kk == 0 and part[0] == 0 and bank_free(m) is not None:
                                    pe.wait_ge(s_free, bank_free(m))
                                last = product(j, kk, m, part)
                                if kk == KT - 1 and part[-1] == 2:
                                    last.then_inc(s_pe[stage], 1)
                    if j < 3:
                        last.then_inc(s_pe[stage], 1)
                    if after is not None:
                        after(4 * g + j)

            def keep_warm(n, bank):
                for _ in range(n):
                    nc.tensor.matmul(ps[:, bank, 0:P], ones, ident, start=True, stop=True)

            def token_sums(norm, bank):
                pe.wait_ge(s_acc, 6 * (norm + 1))
                pe.wait_ge(s_xsq, KT * (norm + 1))
                for t in range(CP):
                    part = slice(t * P, (t + 1) * P)
                    nc.tensor.matmul(ps[:, bank, part], acc[:, part], ones, start=True, stop=False)
                    last = nc.tensor.matmul(ps[:, bank, part], work[1][:, part], ones, start=False, stop=True)
                last.then_inc(s_ss, 1)

            def to_all_partitions(bank, per_token, col):
                for t in range(CP):
                    last = nc.tensor.matmul(ps[:, bank, t * P:(t + 1) * P], per_token[:, col + t:col + t + 1].broadcast_to([P, P]), ident,
                                            start=True, stop=True)
                return last

            def broadcast(norm):
                pe.wait_ge(s_inv, norm + 1)
                to_all_partitions(7, r_tok, 0).then_inc(s_bc, 1)

            def column_sums(tile, start, stop):
                for t in range(CP):
                    last = nc.tensor.matmul(ps[:, t, 0:P], tile[:, t * P:(t + 1) * P], ones, start=start, stop=stop)
                return last

            def post_norm(stage, norm):
                pe.wait_ge(s_free, FREED[stage] + 5)
                pe.wait_ge(s_acc, 6 * (norm + 1))
                column_sums(acc, True, False)
                pe.wait_ge(s_xsq, KT * (norm + 1))
                column_sums(work[1], False, True).then_inc(s_ss, 1)
                keep_warm(WARM_ROOT, 4)
                pe.wait_ge(s_free, FREED[stage] + KT)
                broadcast(norm)
                if norm < 7:
                    keep_warm(WARM_NEXT_H, 4)

            def gla(n):
                if n == 3:
                    pe.wait_ge(s_const, 32)
                    token_sums(0, 6)
                if n == 4:
                    broadcast(0)
                    pe.wait_ge(s_set, 2)
                    for kk in range(KT):
                        last = nc.tensor.matmul(ps[0:RANK, 4, :], w_lr[:, kk, :], x[:, kk, :], start=(kk == 0), stop=(kk == KT - 1))
                    last.then_inc(s_lrp, 1)
                if n == 6:
                    pe.wait_ge(s_lr, 1)
                    pe.wait_ge(s_gk_in, 32)
                    pe.wait_ge(s_rs, 1)
                    for t in range(CP):
                        last = nc.tensor.matmul(ps[:, 4 + t, :], lr[:, t * P:(t + 1) * P], wgk2, start=True, stop=True)
                    last.then_inc(s_gkp, 1)
                if n == 9:
                    pe.wait_ge(s_g, CP)
                    for hd in range(HEADS):
                        for t in range(CP):
                            last = nc.tensor.matmul(ps[:, 4 + hd, t * P:(t + 1) * P], g_tok[:, t, hd * P:(hd + 1) * P], tri,
                                                    start=True, stop=True)
                    last.then_inc(s_bp, 1)
                if n in (11, 12):
                    half = n - 11
                    pe.wait_ge(s_b, 1)
                    pe.wait_ge(s_free, 8)
                    pe.wait_ge(s_qn, HEADS)
                    for hd in (2 * half, 2 * half + 1):
                        for c in range(CP):
                            last = nc.tensor.matmul(ps[:, 4 + hd, c * P:(c + 1) * P], k[:, hd, c * P:(c + 1) * P],
                                                    q[:, hd, c * P:(c + 1) * P], start=True, stop=True)
                    last.then_inc(s_sc, 1)
                if 14 <= n < 14 + LEVELS:
                    lv = n - 14
                    pe.wait_ge(s_qk, 2 * lv + 2)
                    pe.wait_ge(s_pred, lv + 2)
                    for hd in range(HEADS):
                        for c in range(CP):
                            at = (hd * CP + c) * HALF
                            last = nc.tensor.matmul(ps[:, 4 + 2 * (lv % 2) + hd // 2, at % 512:at % 512 + HALF],
                                                    k_lv[:, hd, c * P:(c + 1) * P], q_lv[:, at:at + HALF],
                                                    start=True, stop=True)
                    last.then_inc(s_sc, 1)
                if n == 22:
                    pe.wait_ge(s_qk, 2 * LEVELS + 2)
                    pe.wait_ge(s_pred, LEVELS + 3)
                    for c in range(CP):
                        for hd in range(HEADS):
                            last = nc.tensor.transpose(ps[:, 4 + c, hd * P:(hd + 1) * P], k[:, hd, c * P:(c + 1) * P], ident)
                    last.then_inc(s_kdp, 1)

                if n in (23, 25, 27):
                    c = (n - 23) // 2
                    if c == 0:
                        pe.wait_ge(s_kd, 1)
                        pe.wait_ge(s_free, 16)
                    else:
                        pe.wait_ge(s_state, HEADS * c)
                    for hd in range(HEADS):
                        at = hd * DV
                        last = nc.tensor.matmul(ps[:, 6 + hd // 2, at % 512:at % 512 + DV], kd_tok[:, c, hd * P:(hd + 1) * P],
                                                v[:, c, at:at + DV], start=True, stop=True)
                    last.then_inc(s_u, 1)
                if n in (24, 26, 28, 30):
                    c = (n - 24) // 2
                    if c:
                        pe.wait_ge(s_o, c)
                        pe.wait_ge(s_state, HEADS * c)
                    for hd in range(HEADS):
                        for w in range(2):
                            at = (2 * hd + w) * P
                            bank, at = 4 + at // 512, at % 512
                            col = hd * DV + w * P
                            last = nc.tensor.matmul(ps[:, bank, at:at + P], v[:, c, col:col + P], scores[:, hd * CP + c, :],
                                                    start=True, stop=(c == 0))
                            if c:
                                last = nc.tensor.matmul(ps[:, bank, at:at + P], states[:, c, col:col + P],
                                                        q[:, hd, c * P:(c + 1) * P], start=False, stop=True)
                    last.then_inc(s_op, 1)
                if n == 31:
                    pe.wait_ge(s_oadd, CP)
                    for hd in range(HEADS):
                        for c in range(CP):
                            last = nc.tensor.matmul(ps[:, 4, hd * CP + c:hd * CP + c + 1], v[:, c, hd * DV:hd * DV + P],
                                                    ones[:, 0:1], start=True, stop=True)
                    last.then_inc(s_oss, 1)
                if n == 33:
                    pe.wait_ge(s_ors, 1)
                    for hd in range(HEADS):
                        last = to_all_partitions(4 + hd, ro_tok, hd * CP)
                    last.then_inc(s_obc, 1)

            pe.wait_ge(s_warm_pe, 1)
            for _ in range(WARM_START):
                last = nc.tensor.matmul(ps[:, 0, 0:P], rs[:, 0:P], rs[:, P:2 * P], start=True, stop=True)
            last.then_inc(s_warm_pe, 1)
            for g in range(9):
                narrow_group("in_proj", g, 0, lambda j: 4 * g + j + 1, lambda m: 4 * (g - 1) + m + 1 if g else None,
                             tokens_out=g in (2, 3), after=gla, opening=0 if g == 0 else None)

            def wide_block(stage, k0, banks_free, mlo0, i=None, start=False, stop=False, bank7=None):
                base = FIRST[stage]

                def product(c, m, passes=range(3)):
                    for n in passes:
                        wp, hp = PASSES[n]
                        last = nc.tensor.matmul(ps[:, m, :], wt(c, wp, m * P), m_hl[:, c, hp, :],
                                                start=(start and c == 0 and n == 0), stop=(stop and c == 3 and n == 2))
                    return last

                for c in range(4):
                    if bank7 is not None and c == 0:
                        pe.wait_ge(s_wlo, base + 1)
                        pe.wait_ge(s_mhi, mlo0 + 1)
                        for m in range(7):
                            pe.wait_ge(s_free, banks_free(m))
                            product(c, m, (0, 1))
                        pe.wait_ge(s_mlo, mlo0 + 1)
                        for m in range(7):
                            product(c, m, (2,))
                        pe.wait_ge(*bank7)
                        product(c, 7).then_inc(s_pe[stage], 1)
                        continue
                    if i is None:
                        pe.wait_ge(s_wlo, base + k0 + c + 1)
                        pe.wait_ge(s_mlo, mlo0 + k0 + c + 1)
                    else:
                        pe.wait_ge(s_wlo, i * 4 + (base + c + 1))
                        pe.wait_ge(s_mlo, i * 4 + (mlo0 + c + 1))
                    if stop and c == 2:
                        continue
                    for m in range(8):
                        if start and c == 0 and banks_free(m) is not None:
                            pe.wait_ge(s_free, banks_free(m))
                        if stop and c == 3:
                            product(2, m)
                            product(3, m).then_inc(s_pe[stage], 1)
                        else:
                            last = product(c, m)
                    if not (stop and c == 3):
                        last.then_inc(s_pe[stage], 1)

            pe.wait_ge(s_mid, 2)
            f = FREED["out_proj"]
            wide_block("out_proj", 0, lambda m: f - 4 + m + 1 if m < 4 else None, 0, start=True)
            wide_block("out_proj", 4, None, 0)
            wide_block("out_proj", 8, None, 0, stop=True)
            post_norm("out_proj", 1)

            def mlp(layer):
                up, down = f"up{layer}", f"down{layer}"
                o_idx = 1 if layer == 0 else 3
                u0, d0 = FIRST[up], FIRST[down]
                fu, fd = FREED[up] - 8, FREED[down] - 8
                narrow_group(up, 0, 0, lambda j: u0 + j + 1, lambda m: fu + m + 1, opening=o_idx)
                token_sums(2 * o_idx, 7)
                narrow_group(up, 1, 4, lambda j: u0 + 4 + j + 1, lambda m: fu + 4 + m + 1, norm=2 * o_idx)
                with pe.Fori(1, 4) as i:
                    for half in range(2):
                        narrow_group(up, None, 4 * half, lambda j: i * 8 + (u0 + 4 * half + j + 1),
                                     lambda m: i * 8 + (fu + 4 * half + m + 1))
                mlo0 = SPLIT_DONE[down]
                wide_block(down, 0, lambda m: fd + m + 1, mlo0, start=True)
                with pe.Fori(1, 7) as i:
                    wide_block(down, 0, None, mlo0, i=i)
                wide_block(down, 28, None, mlo0, stop=True)
                post_norm(down, 2 * o_idx + 1)

            mlp(0)

            p0, fp = FIRST["pw1"], FREED["pw1"] - 8
            narrow_group("pw1", 0, 0, lambda j: p0 + j + 1, lambda m: fp + m + 1, opening=2)
            token_sums(4, 7)
            narrow_group("pw1", 1, 4, lambda j: p0 + 4 + j + 1, lambda m: fp + 4 + m + 1, norm=4)
            for g in (2, 3):
                narrow_group("pw1", g, 4 * (g % 2), lambda j: p0 + 4 * g + j + 1,
                             lambda m: FREED["pw1"] + 4 * (g - 2) + GLU_READ[m])

            pe.wait_ge(s_free, FREED["pw1"] + 12)
            for no, (c, t0, n) in enumerate(BATCHES):
                i = c - PE_TILES[0]
                if t0 == 0:
                    pe.wait_ge(s_ulo, i + 1)
                for j, (wp, up_) in enumerate(PASSES):
                    if j < 2:
                        pe.wait_ge((s_diagw, s_diagl)[j], no + 1)
                    for t in range(n):
                        last = nc.tensor.matmul(ps[:, i, :], diag[:, no % 2, wp, t, :], u_hl[:, i, up_, t0 + t:t0 + t + T],
                                                start=(t0 + t == 0 and j == 0), stop=(t0 + t == PE_TAPS[c] - 1 and j == 2))
                last.then_inc(s_tap, 1)

            pe.wait_ge(s_free, FREED["pw2"])
            pe.wait_ge(s_cv, CONV_DVE)
            nc.tensor.matmul(ps[:, 4, :], ones, d[:, 5, :], start=True, stop=False)
            nc.tensor.matmul(ps[:, 4, :], ones, d[:, SUMMED_TILE, :], start=False, stop=False)
            pe.wait_ge(s_dsum, 4)
            nc.tensor.matmul(ps[:, 4, :], ones, acc[:, :], start=False, stop=False)
            pe.wait_ge(s_dpe, 3)
            nc.tensor.matmul(ps[:, 4, :], ones, d[:, 7, :], start=False, stop=True).then_inc(s_mean, 1)
            keep_warm(WARM_MEAN, 5)
            sources = ((0, (s_lnsq, 1)), (1, (s_lnsq, 2)), (2, (s_lnadd, 1)), (4, (s_lnadd, 2)), (6, (s_lnsq, 7)), (7, (s_lnsq, 8)))
            for n, (src, ready) in enumerate(sources):
                pe.wait_ge(*ready)
                last = column_sums(act_d[:, src, :], n == 0, n == len(sources) - 1)
            last.then_inc(s_lnss, 1)
            keep_warm(WARM_ROOT, 5)
            pe.wait_ge(s_lninv, 1)
            to_all_partitions(7, r_tok, 0).then_inc(s_lnbc, 1)
            keep_warm(WARM_SILU, 5)
            f2 = FREED["pw2"] - 8
            m2 = SPLIT_DONE["pw2"]
            wide_block("pw2", 0, lambda m: f2 + m + 1, m2, start=True, bank7=(s_z, KT))
            wide_block("pw2", 4, None, m2, stop=True)
            post_norm("pw2", 5)
            mlp(1)

        @block.vector
        def _(dve):
            def h_low(m, o_idx, gain):
                dve.wait_ge(s_hhi, KT * o_idx + m + 1)
                nc.vector.scalar_tensor_tensor(h_lo[:, m, :], x[:, m, :], gain, h_hi[:, m, :].bitcast(fp32),
                                               ALU.mult, ALU.subtract).then_inc(s_hlo, 1)

            def add_square(m, norm):
                dve.wait_ge(s_xsq, KT * norm + m + 1)
                if m > 1:
                    dve.wait_ge(s_acc, 6 * norm + m - 1)
                nc.vector.tensor_tensor(acc[:, :], acc[:, :], work[m % 2][:, :], ALU.add).then_inc(s_acc, 1)

            def inverse_rms(norm):
                dve.wait_ge(s_sqrt, norm + 1)
                nc.vector.reciprocal(r_tok[:, :], r_tok[:, :]).then_inc(s_inv, 1)

            nc.vector.memset(r_tok[:, :], 0.0).then_inc(s_warm, 1)
            nc.vector.memset(rs[:, :], 0.0).then_inc(s_warm_pe, 1)
            dve.wait_ge(s_vec, 16)
            for m in range(KT):
                h_low(m, 0, vcol("mix_pre", m))
                if 0 < m < KT - 1:
                    add_square(m, 0)
            dve.wait_ge(s_const, 32)
            nc.vector.tensor_copy(mask[:, :], mask_in)
            nc.vector.memset(lr, 1.0).then_inc(s_set, 1)
            dve.wait_ge(s_lr_in, 16)
            for kk in range(KT):
                last = nc.vector.tensor_scalar(w_lr[:, kk, :], w_lr[:, kk, :], vcol("mix_pre", kk), None, ALU.mult)
            last.then_inc(s_set, 1)

            def evac(stage, g, m, out, bank0):
                dve.wait_ge(s_pe[stage], narrow_bank_done(g, m))
                return nc.vector.tensor_tensor(out, ps[:, bank0 + m, :], rs[:, :], ALU.mult).then_inc(s_free, 1)

            def halves(t, s):
                return t.rearrange("p (c s) -> p c s", s=s)

            flat = lambda t: t[:, :, :].rearrange("p a n -> p (a n)")

            def at_level(lv):
                s = CHUNK >> lv
                return s, s // 2, halves(flat(b), s), halves(flat(k), s), halves(flat(q), s), halves(k_lv.rearrange("p a n -> p (a n)"), s)

            for n in range(37):
                if n == 4:
                    for m in range(4):
                        dve.wait_ge(s_pe["in_proj"], narrow_bank_done(0, m))
                        nc.vector.tensor_copy(q[:, m, :], ps[:, m, :]).then_inc(s_free, 1)
                    inverse_rms(0)
                if n == 5:
                    dve.wait_ge(s_rs, 1)
                    dve.wait_ge(s_free, HEADS)
                    for m in range(4):
                        nc.vector.scalar_tensor_tensor(q[:, m, :], q[:, m, :], float(DK) ** -0.5, rs[:, :],
                                                       ALU.mult, ALU.mult).then_inc(s_qn, 1)
                    dve.wait_ge(s_lrp, 1)
                    dve.wait_ge(s_set, 1)
                    nc.vector.tensor_tensor(lr[0:RANK, :], ps[0:RANK, 4, :], rs[0:RANK, :], ALU.mult).then_inc(s_lr, 1)
                    nc.vector.memset(scores, 0.0).then_inc(s_pred, 1)
                if n == 8:
                    for m in range(4):
                        evac("in_proj", 1, m, k[:, m, :], 0)
                    for t in range(CP):
                        dve.wait_ge(s_sp, 3)
                        nc.vector.scalar_tensor_tensor(g_tok[:, t, :], ps[:, 4 + t, :], 0.0, softp[:, t, :],
                                                       ALU.min, ALU.subtract).then_inc(s_g, 1)
                if n in (12, 16):
                    for m in range(4):
                        c = 512 * (n == 16)
                        dve.wait_ge(s_pe["in_proj"], narrow_bank_done(n // 4 - 1, m))
                        nc.vector.tensor_scalar(v[:, m, c:c + 512], ps[:, m, :], r_tok[:, m:m + 1], None, ALU.mult).then_inc(s_free, 1)
                if n in (20, 24):
                    for m in range(4):
                        c = m + 4 * (n == 24)
                        evac("in_proj", n // 4 - 1, m, gate[:, c, :], 0)
                if n == 28:
                    for m in range(4):
                        evac("in_proj", 6, m, y_a[:, m, :], 0)
                if n == 32:
                    for m in range(4):
                        evac("in_proj", 7, m, sc_p[:, m, :], 0)
                if n == 33:
                    dve.wait_ge(s_free, 32)
                    nc.vector.tensor_tensor(sc_p[:, :, :], sc_p[:, :, :], y_a[:, :, :], ALU.mult).then_inc(s_scv, 1)

                if n in (12, 13):
                    half = n - 12
                    dve.wait_ge(s_sc, half + 1)
                    dve.wait_ge(s_pred, 1 + half)
                    dm = mask[:, LEVELS * HALF:].rearrange("p (a i) -> p a i", a=1).broadcast_to([P, 8, P])
                    nc.vector.copy_predicated(scores[:, 8 * half:8 * half + 8, :], dm,
                                              ps[:, 4 + 2 * half:6 + 2 * half, :].rearrange("p a (c i) -> p (a c) i", i=P)).then_inc(s_pred, 1)
                lv = n - 14
                if 0 <= lv < LEVELS:
                    s, hf, _, kk_, qq, kl = at_level(lv)
                    ee = halves(e_lv, s)
                    dve.wait_ge(s_exp, lv + 1)
                    if lv:
                        dve.wait_ge(s_sc, 2 + lv)
                    nc.vector.scalar_tensor_tensor(halves(q_lv, hf), ee[:, :, hf:], 1.0, qq[:, :, hf:], ALU.min, ALU.mult).then_inc(s_qk, 1)
                    nc.vector.scalar_tensor_tensor(kl[:, :, :hf], ee[:, :, :hf], 1.0, kk_[:, :, :hf], ALU.min, ALU.mult).then_inc(s_qk, 1)
                lp = n - 15
                if 0 <= lp < LEVELS:
                    blk = CHUNK >> lp
                    second = blk // 2
                    dve.wait_ge(s_sc, 2 + lp + 1)
                    dve.wait_ge(s_pred, 3 + lp)
                    for bank in range(2):
                        dst = scores[:, 8 * bank:8 * bank + 8, :].rearrange("p c (b s) -> p c b s", s=blk)[:, :, :, second:]
                        src = ps[:, 4 + 2 * (lp % 2) + bank, :].rearrange("p (c b i) -> p c b i", c=8, i=second)
                        mk = mask[:, lp * HALF:(lp + 1) * HALF].rearrange("p (a b i) -> p a b i", a=1, i=second).broadcast_to([P, 8, HALF // second, second])
                        last = nc.vector.copy_predicated(dst, mk, src)
                    last.then_inc(s_pred, 1)
                lv = n - 13
                if 0 <= lv < LEVELS:
                    s, hf, bb, _, _, _ = at_level(lv)
                    ee = halves(e_lv, s)
                    ref = bb[:, :, hf - 1:hf].broadcast_to([P, HEADS * T // s, hf])
                    dve.wait_ge(s_b, 1)
                    if lv:
                        dve.wait_ge(s_qk, 2 * lv)
                    nc.vector.tensor_tensor(ee[:, :, hf:], bb[:, :, hf:], ref, ALU.subtract).then_inc(s_e, 1)
                    nc.vector.tensor_tensor(ee[:, :, :hf], ref, bb[:, :, :hf], ALU.subtract).then_inc(s_e, 1)
                if n == 21:
                    dve.wait_ge(s_exp, LEVELS + 1)
                    nc.vector.scalar_tensor_tensor(flat(q), e_lv, 1.0, flat(q), ALU.min, ALU.mult).then_inc(s_qk, 1)
                    bb = halves(flat(b), CHUNK)
                    last_b = bb[:, :, CHUNK - 1:CHUNK].broadcast_to([P, HEADS * T // CHUNK, CHUNK])
                    dve.wait_ge(s_qk, 2 * LEVELS + 1)
                    nc.vector.tensor_tensor(halves(e_lv, CHUNK), last_b, bb, ALU.subtract).then_inc(s_e, 1)
                if n == 22:
                    dve.wait_ge(s_exp, LEVELS + 2)
                    nc.vector.scalar_tensor_tensor(flat(k), e_lv, 1.0, flat(k), ALU.min, ALU.mult).then_inc(s_qk, 1)
                if n in (24, 26, 28):
                    c = (n - 24) // 2
                    dve.wait_ge(s_u, c + 1)
                    dve.wait_ge(s_el, 1)
                    if c:
                        dve.wait_ge(s_state, HEADS * c)
                    for hd in range(HEADS):
                        at = hd * DV
                        new = states[:, c + 1, at:at + DV]
                        src = ps[:, 6 + hd // 2, at % 512:at % 512 + DV]
                        if c == 0:
                            nc.vector.tensor_copy(new, src).then_inc(s_state, 1)
                        else:
                            nc.vector.scalar_tensor_tensor(new, states[:, c, at:at + DV], e_last[:, hd, c:c + 1], src,
                                                           ALU.mult, ALU.add).then_inc(s_state, 1)
                heads_of = lambda t: t.rearrange("p (h w) n -> p h w n", w=2)
                if n in (26, 28, 30, 31):
                    c = (26, 28, 30, 31).index(n)
                    dve.wait_ge(s_osq, c + 1)
                    sq = heads_of(v[:, c, :].rearrange("p (a n) -> p a n", n=P))
                    nc.vector.tensor_tensor(sq[:, :, 0, :], sq[:, :, 0, :], sq[:, :, 1, :], ALU.add).then_inc(s_oadd, 1)
                if n == 32:
                    dve.wait_ge(s_osqrt, 1)
                    nc.vector.reciprocal(ro_tok[:, :], ro_tok[:, :]).then_inc(s_ors, 1)
                if n == 33:
                    dve.wait_ge(s_silu, 8)
                    for w in range(2):
                        nc.vector.scalar_tensor_tensor(heads_of(gate[:, :, :])[:, :, w, :], heads_of(o[:, :, :])[:, :, w, :],
                                                       vcol("gla_g", w), heads_of(gate[:, :, :])[:, :, w, :],
                                                       ALU.mult, ALU.mult).then_inc(s_og, 1)
                if n == 34:
                    dve.wait_ge(s_obc, 1)
                    dve.wait_ge(s_og, 2)
                    for half in range(2):
                        rs_heads = ps[:, 4 + 2 * half:6 + 2 * half, :].rearrange("p h (w n) -> p h w n", w=1).broadcast_to([P, 2, 2, T])
                        nc.vector.tensor_tensor(heads_of(o[:, 4 * half:4 * half + 4, :]), heads_of(gate[:, 4 * half:4 * half + 4, :]),
                                                rs_heads, ALU.mult).then_inc(s_mid, 1)

            def m_low(src, kk, mhi_no):
                dve.wait_ge(s_mhi, mhi_no)
                nc.vector.tensor_tensor(m_hl[:, kk % RING, 1, :], src, m_hl[:, kk % RING, 0, :].bitcast(fp32),
                                        ALU.subtract).then_inc(s_mlo, 1)

            def short_conv(m):
                wc = lambda tap: vcol("w_sc", tap * 4 + m)
                dve.wait_ge(s_scv, 1)
                nc.vector.tensor_scalar(y_a[:, m, :], sc_p[:, m, :], wc(2), None, ALU.mult).then_inc(s_scv, 1)
                dve.wait_ge(s_scv, 3 * m + 2)
                nc.vector.scalar_tensor_tensor(y_a[:, m, 1:], sc_p[:, m, :T - 1], wc(1), y_a[:, m, 1:], ALU.mult, ALU.add).then_inc(s_scv, 1)
                dve.wait_ge(s_scv, 3 * m + 3)
                nc.vector.scalar_tensor_tensor(y_a[:, m, 2:], sc_p[:, m, :T - 2], wc(0), y_a[:, m, 2:], ALU.mult, ALU.add).then_inc(s_scv, 1)
                dve.wait_ge(s_scv, 3 * m + 4)
                nc.vector.tensor_tensor(y_a[:, m, :], y_a[:, m, :], q[:, m, :], ALU.mult).then_inc(s_mid, 1)

            for kk in range(3):
                m_low(o[:, kk, :], kk, kk + 1)
            for m in range(4):
                evac("in_proj", 8, m, q[:, m, :], 0)
            dve.wait_ge(s_free, 36)
            short_conv(0)
            short_conv(1)
            m_low(o[:, 3, :], 3, 4)
            short_conv(2)
            short_conv(3)
            for kk in range(4, 8):
                m_low(o[:, kk, :], kk, kk + 1)
            for kk in range(8, 12):
                m_low(y_a[:, kk - 8, :], kk, kk + 1)

            def close(stage, o_idx, gain, gain0, pre, pre0, bias):
                post = 2 * o_idx - 1
                for m in range(KT):
                    if 1 <= m < KT - 1:
                        add_square(m, post)
                    dve.wait_ge(s_xsq, KT * post + m + 1)
                    nc.vector.tensor_scalar(y[:, m, :], ps[:, m, :], vcol(bias, m) if bias else 0.0, vcol(gain, gain0 + m),
                                            ALU.add, ALU.mult).then_inc(s_free, 1)
                inverse_rms(post)
                if o_idx == 1:
                    dve.wait_ge(s_x_again, 16)
                dve.wait_ge(s_bc, post + 1)
                for m in range(KT):
                    nc.vector.tensor_tensor(y[:, m, :], y[:, m, :], ps[:, 7, :], ALU.mult).then_inc(s_yn, 1)
                    if not pre and m in LAST_POOL:
                        continue
                    dve.wait_ge(s_yn, KT * (o_idx - 1) + m + 1)
                    nc.vector.tensor_tensor(x[:, m, :], x[:, m, :], y[:, m, :], ALU.add).then_inc(s_xnew, 1)
                    if pre and m:
                        h_low(m - 1, o_idx, vcol(pre, pre0 + m - 1))
                        if m > 1:
                            add_square(m - 1, 2 * o_idx)
                if pre:
                    h_low(KT - 1, o_idx, vcol(pre, pre0 + KT - 1))

            def mlp(layer):
                up, down = f"up{layer}", f"down{layer}"
                o_idx = 1 if layer == 0 else 3
                mid_done, mhi0 = MID_DONE[down], SPLIT_DONE[down]
                f_up = FREED[up]

                def evac_group(half, i=None, tile0=0):
                    at = (lambda c, per: c) if i is None else (lambda c, per: i * per + c)
                    g0 = tile0 // 4
                    for m in range(4):
                        dve.wait_ge(s_pe[up], at(narrow_bank_done(g0, m), 14))
                        nc.vector.tensor_tensor(work[m % 2][:, :], ps[:, 4 * half + m, :], rs[:, :], ALU.mult).then_inc(s_free, 1)
                        dve.wait_ge(s_free, at(f_up + tile0 + m + 1, 8))
                        dst = mid[:, tile0 + m, :] if i is None else mid[:, bass.ds(i * 8 + (tile0 + m), 1), :].rearrange("p a n -> p (a n)")
                        nc.vector.scalar_tensor_tensor(dst, work[m % 2][:, :], 0.0, work[m % 2][:, :],
                                                       ALU.max, ALU.mult).then_inc(s_mid, 1)

                inverse_rms(2 * o_idx)
                dve.wait_ge(s_rs, o_idx + 1)
                evac_group(0)
                evac_group(1, tile0=4)
                for kk in range(3):
                    m_low(mid[:, kk, :], kk, mhi0 + kk + 1)
                with dve.Fori(1, 4) as i:
                    evac_group(0, i, 0)
                    evac_group(1, i, 4)
                m_low(mid[:, 3, :], 3, mhi0 + 4)
                with dve.Fori(1, 8) as i:
                    for c in range(4):
                        dve.wait_ge(s_mhi, i * 4 + (mhi0 + c + 1))
                        nc.vector.tensor_tensor(m_hl[:, c, 1, :], mid[:, bass.ds(i * 4 + c, 1), :].rearrange("p a n -> p (a n)"),
                                                m_hl[:, c, 0, :].bitcast(fp32), ALU.subtract).then_inc(s_mlo, 1)
                if layer == 0:
                    close(down, 2, "mlp_post", 0, "mix_pre", KT, None)
                else:
                    close(down, 4, "mlp_post", KT, None, 0, None)

            close("out_proj", 1, "mix_post", 0, "mlp_pre", 0, None)
            mlp(0)

            nc.vector.memset(u[:, :, 0:CF_K - 1], 0.0).then_inc(s_uw, 1)
            inverse_rms(4)
            f = FREED["pw1"]

            def glu(g):
                bank0 = 4 * (g % 2)
                if g:
                    dve.wait_ge(s_u1, 2 * g)
                for m in (2, 3, 0, 1):
                    dve.wait_ge(s_pe["pw1"], narrow_bank_done(g, m))
                    out = sg[:, m - 2, :] if m >= 2 else work[m][:, :]
                    nc.vector.tensor_tensor(out, ps[:, bank0 + m, :], rs[:, :], ALU.mult).then_inc(s_free, 1)
                for m in range(2):
                    c = 2 * g + m
                    dve.wait_ge(s_free, f + 4 * g + 2 + m + 1)
                    dve.wait_ge(s_sig, c + 1)
                    nc.vector.scalar_tensor_tensor(u[:, c, CF_K - 1:], work[m][:, :], vcol("b_pw1", c), sg[:, m, :],
                                                   ALU.add, ALU.mult).then_inc(s_u1, 1)

            def first_taps(tiles):
                dve.wait_ge(s_uw, 1)
                dve.wait_ge(s_u1, tiles[1] + 1)
                for t in tiles:
                    nc.vector.tensor_scalar(d[:, t, :], u[:, t, 0:T], vcol("w_dw", t * CF_K), vcol("b_dw", t),
                                            ALU.mult, ALU.add).then_inc(s_cv, 1)

            def taps(tiles, t0, t1, done):
                n = len(tiles)
                with dve.Fori(t0, t1) as i:
                    for k, t in enumerate(tiles):
                        at = dve.snap(i + (VEC["w_dw"] + t * CF_K))
                        dve.wait_ge(s_cv, i * n + (done - n * t0 + k + 1 - n))
                        nc.vector.scalar_tensor_tensor(d[:, t, :], u[:, t, bass.ds(i, T)], vec[:, bass.ds(at, 1)],
                                                       d[:, t, :], ALU.mult, ALU.add).then_inc(s_cv, 1)

            lo0 = PE_TILES[0] * CF_K
            dve.wait_ge(s_dwhi, 1)
            nc.vector.tensor_tensor(dw_lo[:, :], vec[:, VEC["w_dw"] + lo0:VEC["w_dw"] + KT * CF_K],
                                    dw_hi[:, :].bitcast(fp32), ALU.subtract).then_inc(s_dwlo, 1)
            dve.wait_ge(s_rs, 3)
            glu(0)
            first_taps((0, 1))
            taps((0, 1), 1, 13, 2)
            glu(1)
            taps((0, 1), 13, 25, 26)
            glu(2)
            taps((0, 1), 25, CF_K, 50)
            first_taps((2, 4))
            taps((2, 4), 1, 4, DONE01 + 2)
            glu(3)
            taps((2, 4), 4, CF_K, DONE01 + 8)
            dve.wait_ge(s_dpe, 1)
            dve.wait_ge(s_padd, SUMMED_TAPS - 1)
            taps((5, SUMMED_TILE), SUMMED_TAPS, CF_K, DONE24)

            dve.wait_ge(s_mean, 1)
            for m in range(KT):
                nc.vector.scalar_tensor_tensor(d[:, m, :], ps[:, 4, :], -1.0 / D, d[:, m, :], ALU.mult, ALU.add).then_inc(s_ln, 1)
            dve.wait_ge(s_lnroot, 1)
            nc.vector.reciprocal(r_tok[:, :], r_tok[:, :]).then_inc(s_lninv, 1)
            dve.wait_ge(s_lnbc, 1)
            for m in range(KT):
                nc.vector.tensor_tensor(d[:, m, :], d[:, m, :], ps[:, 7, :], ALU.mult).then_inc(s_z, 1)
                if m >= 5:
                    m_low(act_d[:, m - 5, :], m - 5, SPLIT_DONE["pw2"] + m - 4)
            for m in range(KT - 5, KT):
                m_low(act_d[:, m, :], m, SPLIT_DONE["pw2"] + m + 1)
            close("pw2", 3, "mix_post", KT, "mlp_pre", KT, "b_pw2")
            mlp(1)


_INS = ["x_t", "w_in", "w_gk2", "b_gk2", "w_out", "w_pw1", "w_pw2", "w_up", "w_down", "vecs", "squares", "masks"]


def _columns(a):
    return np.ascontiguousarray(a.reshape(-1, P).T)


def _shape_constants():
    j, i = np.arange(P)[:, None], np.arange(P)[None, :]
    tri = (j <= i) / GATE_NORM
    squares = np.stack([np.ones((P, P)), np.eye(P), tri], axis=1).astype(np.float32)
    levels = []
    for lv in range(LEVELS):
        s = CHUNK >> lv
        n = np.arange(HALF)
        row = (n // (s // 2)) * s + s // 2 + n % (s // 2)
        levels.append((j // s == row // s) & (j % s < s // 2))
    return squares, np.concatenate([*levels, j == i], axis=1).astype(np.float32)


def kernel(**inputs):
    import concourse.bacc as bacc
    from concourse.bass_utils import run_bass_kernel_spmd

    a = {n: np.asarray(t) for n, t in inputs.items()}
    squares, masks = _shape_constants()
    dw = a["cf_w_dw"][0].reshape(CF_K, KT, P).transpose(1, 0, 2).reshape(-1)
    parts = [a["norm_mix_pre"], a["norm_mix_post"], a["norm_mlp_pre"], a["norm_mlp_post"], a["cf_b_pw1"], a["cf_b_dw"],
             a["cf_ln_g"], a["cf_ln_b"], a["cf_b_pw2"], a["gla_norm_g"], a["sc_w_conv"], dw]
    cols = [_columns(p) for p in parts]
    cols += [np.full((P, 1), EPS, np.float32)]
    pw1 = a["cf_w_pw1"][0].reshape(D, 2, 4, D // 4).transpose(0, 2, 1, 3).reshape(D, 2 * D)
    arrays = {"x_t": a["x"][0].T, "w_in": a["ab_w_in"][0], "w_gk2": a["gla_w_gk2"][0], "b_gk2": a["gla_b_gk2"],
              "w_out": a["ab_w_out"][0], "w_pw1": pw1, "w_pw2": a["cf_w_pw2"][0],
              "w_up": a["mlp_w1"], "w_down": a["mlp_w2"], "vecs": np.concatenate(cols, axis=1),
              "squares": squares, "masks": masks}
    arrays = {n: np.ascontiguousarray(t) for n, t in arrays.items()}
    nc = bacc.Bacc("TRN2", target_bir_lowering=False, num_devices=1)
    args = [nc.dram_tensor(n, arrays[n].shape, mybir.dt.from_np(arrays[n].dtype), kind="ExternalInput").ap() for n in _INS]
    out_t = nc.dram_tensor("out_t", (D, T), mybir.dt.float32, kind="ExternalOutput").ap()
    build(nc, *args, out_t)
    r = run_bass_kernel_spmd(nc, [arrays], core_ids=[0])
    return np.ascontiguousarray(np.asarray(r.results[0]["out_t"]).T)[None]
```
